# Optimizing a Trainium2 kernel written in Bass

```python
import jax, jax.numpy as jnp
from jax import lax
import numpy as np

D_MODEL = 1024
BATCH = 1
SEQ = 512
DEPTH = 2
DEC_BATCH = 1
DEC_SEQ = 32
PAST_LEN = 128

CHUNK = 64
Q_BLOCK = 128
N_MEM = 256
EPS = 1e-5
ALPHA = (2 * DEPTH) ** 0.25
BETA = (8 * DEPTH) ** -0.25

POOL_WINDOWS = (2, 4, 8, 16)
POOL_GROUP = D_MODEL // 16
POOL_WIDTH = len(POOL_WINDOWS) * POOL_GROUP
POOL_HIST = max(POOL_WINDOWS) - 1

MLA_HEADS = 8
MLA_Q_RANK = D_MODEL // 4
MLA_KV_RANK = D_MODEL // 4
MLA_NOPE = 64
MLA_ROPE = 32
MLA_V = 64
MLA_SCALE = (MLA_NOPE + MLA_ROPE) ** -0.5
ROPE_BASE = 10000.0

GLA_HEADS = 4
GLA_DK = 32
GLA_DV = 64
GLA_GATE_RANK = 16
GLA_GATE_TAU = 16.0

MEM_HEADS = 4
MEM_HEAD_DIM = D_MODEL // MEM_HEADS
D_FF = 2816

IN_SPLITS = (POOL_WIDTH, MLA_Q_RANK, MLA_KV_RANK, MLA_ROPE,
             GLA_HEADS * GLA_DK, GLA_HEADS * GLA_DK, GLA_HEADS * GLA_DV,
             GLA_GATE_RANK, GLA_HEADS * GLA_DV, 3 * D_MODEL)
IN_COLS = sum(IN_SPLITS)

kernel_name = 'hybrid_streaming_encoder_step'

def layer_norm(x, g, b):
    xf = x.astype(jnp.float32)
    mu = jnp.mean(xf, -1, keepdims=True)
    var = jnp.mean(jnp.square(xf - mu), -1, keepdims=True)
    return ((xf - mu) * lax.rsqrt(var + EPS) * g + b).astype(x.dtype)

def rms_norm(x, g):
    xf = x.astype(jnp.float32)
    return (xf * lax.rsqrt(jnp.mean(xf * xf, -1, keepdims=True) + EPS) * g).astype(x.dtype)

def swiglu(x, w_in, w_out):
    gate, up = jnp.split(x @ w_in, 2, axis=-1)
    return (jax.nn.silu(gate) * up) @ w_out

def split_in(h):
    idx, acc = [], 0
    for w in IN_SPLITS[:-1]:
        acc += w
        idx.append(acc)
    return jnp.split(h, idx, axis=-1)

def rope(x, pos):
    half = MLA_ROPE // 2
    inv = ROPE_BASE ** (-jnp.arange(half, dtype=jnp.float32) / half)
    ang = pos.astype(jnp.float32)[:, None] * inv
    cos = jnp.cos(ang)[:, None, :]
    sin = jnp.sin(ang)[:, None, :]
    xf = x.astype(jnp.float32)
    x1, x2 = xf[..., :half], xf[..., half:]
    return jnp.concatenate([x1 * cos - x2 * sin, x2 * cos + x1 * sin], -1).astype(x.dtype)

def pool_mixer(u, hist, pos, pool_w, pool_scale):
    B, S, _ = u.shape
    ext = jnp.concatenate([hist, u], 1).astype(jnp.float32)
    cs = jnp.pad(jnp.cumsum(ext, axis=1), ((0, 0), (1, 0), (0, 0)))
    outs = []
    for gi, w in enumerate(POOL_WINDOWS):
        sl = slice(gi * POOL_GROUP, (gi + 1) * POOL_GROUP)
        hi = cs[:, POOL_HIST + 1:, sl]
        lo = cs[:, POOL_HIST + 1 - w:POOL_HIST + 1 - w + S, sl]
        cnt = jnp.minimum(pos + 1, w).astype(jnp.float32)[None, :, None]
        outs.append((hi - lo) / cnt)
    pooled = jnp.concatenate(outs, -1) - ext[:, POOL_HIST:]
    pooled = pooled.reshape(B, S, len(POOL_WINDOWS), POOL_GROUP)
    y = jnp.einsum('bsgc,gcd->bsgd', pooled, pool_w).reshape(B, S, POOL_WIDTH) * pool_scale
    return y.astype(u.dtype), ext[:, -POOL_HIST:].astype(u.dtype)

def mla_attend(q_abs, q_rope, ckv, kr, mask):
    s = jnp.einsum('bqhc,bkc->bhqk', q_abs, ckv) + jnp.einsum('bqhr,bkr->bhqk', q_rope, kr)
    s = s.astype(jnp.float32) * MLA_SCALE
    if mask is not None:
        s = jnp.where(mask, s, -jnp.inf)
    p = jax.nn.softmax(s, axis=-1).astype(ckv.dtype)
    return jnp.einsum('bhqk,bkc->bqhc', p, ckv)

def mla_prompt_attend(q_abs, q_rope, ckv, kr):
    B, S = q_abs.shape[:2]
    nb = S // Q_BLOCK
    qa = q_abs.reshape(B, nb, Q_BLOCK, MLA_HEADS, MLA_KV_RANK).swapaxes(0, 1)
    qr = q_rope.reshape(B, nb, Q_BLOCK, MLA_HEADS, MLA_ROPE).swapaxes(0, 1)
    key_chunk = jnp.arange(S) // CHUNK

    def blk(args):
        i, qa_i, qr_i = args
        q_chunk = (i * Q_BLOCK + jnp.arange(Q_BLOCK)) // CHUNK
        return mla_attend(qa_i, qr_i, ckv, kr, key_chunk[None, :] <= q_chunk[:, None])

    lat = lax.map(blk, (jnp.arange(nb), qa, qr))
    return lat.swapaxes(0, 1).reshape(B, S, MLA_HEADS, MLA_KV_RANK)

def gla_block(S0, xs):
    q, k, v, la = xs
    C = q.shape[2]
    b = jnp.cumsum(la, axis=2)
    o_inter = jnp.einsum('bhtk,bhkv->bhtv', q * jnp.exp(b), S0)
    causal = jnp.tril(jnp.ones((C, C), bool))[:, :, None]
    diff = b[:, :, :, None, :] - b[:, :, None, :, :]
    decay = jnp.exp(jnp.where(causal, diff, -jnp.inf))
    A = jnp.einsum('bhtk,bhtsk,bhsk->bhts', q, decay, k)
    o = o_inter + jnp.einsum('bhts,bhsv->bhtv', A, v)
    bC = b[:, :, -1]
    S_new = jnp.exp(bC)[..., None] * S0 + jnp.einsum('bhsk,bhsv->bhkv', k * jnp.exp(bC[:, :, None] - b), v)
    return S_new, o

def gla_mixer(gq, gk, gv, ga, gr, S0, w_a2, b_a, norm_g):
    B, S, _ = gq.shape
    f32 = jnp.float32

    def heads(t, d):
        return t.reshape(B, S, GLA_HEADS, d).transpose(0, 2, 1, 3).astype(f32)

    q = heads(gq, GLA_DK) * GLA_DK ** -0.5
    k = heads(gk, GLA_DK)
    v = heads(gv, GLA_DV)
    la = heads(jax.nn.log_sigmoid((ga @ w_a2 + b_a).astype(f32)) / GLA_GATE_TAU, GLA_DK)
    C = min(S, CHUNK)
    nc = S // C

    def to_blocks(t):
        return t.reshape(B, GLA_HEADS, nc, C, t.shape[-1]).transpose(2, 0, 1, 3, 4)

    S_fin, o = lax.scan(gla_block, S0.astype(f32), (to_blocks(q), to_blocks(k), to_blocks(v), to_blocks(la)))
    o = o.transpose(1, 2, 0, 3, 4).reshape(B, GLA_HEADS, S, GLA_DV).transpose(0, 2, 1, 3)
    o = rms_norm(o, norm_g).reshape(B, S, GLA_HEADS * GLA_DV)
    y = o * jax.nn.silu(gr.astype(f32))
    return y.astype(gq.dtype), S_fin.astype(gq.dtype)

def token_mixing(x, pos0, pool_hist, gla_state, ckv_past, kr_past, lw):
    B, S, _ = x.shape
    pos = pos0 + jnp.arange(S)
    u_pool, q_lat, c_kv, kr_raw, gq, gk, gv, ga, gr, gates = split_in(x @ lw['w_in'])
    y_pool, new_pool = pool_mixer(u_pool, pool_hist, pos, lw['pool_w'], lw['pool_scale'])
    q = (rms_norm(q_lat, lw['mla_q_norm']) @ lw['mla_w_uq']).reshape(B, S, MLA_HEADS, MLA_NOPE + MLA_ROPE)
    q_nope, q_rope = q[..., :MLA_NOPE], rope(q[..., MLA_NOPE:], pos)
    q_abs = jnp.einsum('bshn,chn->bshc', q_nope, lw['mla_w_uk'])
    ckv = rms_norm(c_kv, lw['mla_kv_norm'])
    kr = rope(kr_raw[:, :, None, :], pos)[:, :, 0]
    if ckv_past is None:
        lat = mla_prompt_attend(q_abs, q_rope, ckv, kr)
    else:
        lat = mla_attend(q_abs, q_rope, jnp.concatenate([ckv_past, ckv], 1),
                         jnp.concatenate([kr_past, kr], 1), None)
    y_mla = jnp.einsum('bshc,chv->bshv', lat, lw['mla_w_uv']).reshape(B, S, MLA_HEADS * MLA_V)
    y_gla, new_gla = gla_mixer(gq, gk, gv, ga, gr, gla_state, lw['gla_w_a2'], lw['gla_b_a'], lw['gla_norm'])
    g_a, g_b, g_c = jnp.split(jax.nn.sigmoid(gates), 3, axis=-1)
    m = g_a * (y_pool @ lw['w_branch_pool']) + g_b * (y_mla @ lw['w_branch_mla']) + g_c * (y_gla @ lw['w_branch_gla'])
    return m @ lw['w_out'], new_pool, ckv, kr, new_gla

def memory_kv(mem, w_k, w_v):
    B, M, _ = mem.shape
    k = (mem @ w_k).reshape(B, M, MEM_HEADS, MEM_HEAD_DIM)
    v = (mem @ w_v).reshape(B, M, MEM_HEADS, MEM_HEAD_DIM)
    return k, v

def memory_attend(x, k, v, w_q, w_o):
    B, S, _ = x.shape
    q = (x @ w_q).reshape(B, S, MEM_HEADS, MEM_HEAD_DIM)
    s = jnp.einsum('bqhd,bkhd->bhqk', q, k).astype(jnp.float32) * MEM_HEAD_DIM ** -0.5
    p = jax.nn.softmax(s, axis=-1).astype(v.dtype)
    o = jnp.einsum('bhqk,bkhd->bqhd', p, v).reshape(B, S, D_MODEL)
    return o @ w_o

def trunk_layer(x, pos0, pool_hist, gla_state, ckv_past, kr_past, mem_k, mem_v, lw):
    g, b = lw['ln_g'], lw['ln_b']
    x = layer_norm(ALPHA * x + 0.5 * swiglu(x, lw['w_ffn1_in'], lw['w_ffn1_out']), g[0], b[0])
    mix, new_pool, ckv, kr, new_gla = token_mixing(x, pos0, pool_hist, gla_state, ckv_past, kr_past, lw)
    x = layer_norm(ALPHA * x + mix, g[1], b[1])
    x = layer_norm(ALPHA * x + memory_attend(x, mem_k, mem_v, lw['mem_w_q'], lw['mem_w_o']), g[2], b[2])
    x = layer_norm(ALPHA * x + 0.5 * swiglu(x, lw['w_ffn2_in'], lw['w_ffn2_out']), g[3], b[3])
    return x, new_pool, ckv, kr, new_gla

def setup_inputs(seed: int = 0) -> dict:
    key = jax.random.key(seed)
    ks = iter(jax.random.split(key, 48))
    L, D = DEPTH, D_MODEL

    def nrm(shape, scale=1.0):
        return jax.random.normal(next(ks), shape, jnp.float32) * scale

    inp = {}
    inp['x_prompt'] = nrm((BATCH, SEQ, D))
    inp['x_sample'] = nrm((DEC_BATCH, DEC_SEQ, D))
    inp['mem_prompt'] = nrm((BATCH, N_MEM, D))
    inp['cache_pool'] = nrm((L, DEC_BATCH, POOL_HIST, POOL_WIDTH))
    inp['cache_mla_ckv'] = nrm((L, DEC_BATCH, PAST_LEN, MLA_KV_RANK))
    inp['cache_mla_krope'] = nrm((L, DEC_BATCH, PAST_LEN, MLA_ROPE))
    inp['state_gla'] = nrm((L, DEC_BATCH, GLA_HEADS, GLA_DK, GLA_DV), 0.5)
    inp['cache_mem_k'] = nrm((L, DEC_BATCH, N_MEM, MEM_HEADS, MEM_HEAD_DIM))
    inp['cache_mem_v'] = nrm((L, DEC_BATCH, N_MEM, MEM_HEADS, MEM_HEAD_DIM))
    inp['ln_g'] = 1.0 + nrm((L, 4, D), 0.02)
    inp['ln_b'] = nrm((L, 4, D), 0.02)
    inp['w_ffn1_in'] = nrm((L, D, 2 * D_FF), D ** -0.5)
    inp['w_ffn1_out'] = nrm((L, D_FF, D), BETA * D_FF ** -0.5)
    inp['w_in'] = nrm((L, D, IN_COLS), D ** -0.5)
    inp['pool_w'] = nrm((L, len(POOL_WINDOWS), POOL_GROUP, POOL_GROUP), POOL_GROUP ** -0.5)
    inp['pool_scale'] = 1.0 + nrm((L, POOL_WIDTH), 0.02)
    inp['mla_q_norm'] = 1.0 + nrm((L, MLA_Q_RANK), 0.02)
    inp['mla_kv_norm'] = 1.0 + nrm((L, MLA_KV_RANK), 0.02)
    inp['mla_w_uq'] = nrm((L, MLA_Q_RANK, MLA_HEADS * (MLA_NOPE + MLA_ROPE)), MLA_Q_RANK ** -0.5)
    inp['mla_w_uk'] = nrm((L, MLA_KV_RANK, MLA_HEADS, MLA_NOPE), MLA_KV_RANK ** -0.5)
    inp['mla_w_uv'] = nrm((L, MLA_KV_RANK, MLA_HEADS, MLA_V), MLA_KV_RANK ** -0.5)
    inp['gla_w_a2'] = nrm((L, GLA_GATE_RANK, GLA_HEADS * GLA_DK), GLA_GATE_RANK ** -0.5)
    inp['gla_b_a'] = nrm((L, GLA_HEADS * GLA_DK), 0.1)
    inp['gla_norm'] = 1.0 + nrm((L, GLA_DV), 0.02)
    inp['w_branch_pool'] = nrm((L, POOL_WIDTH, D), POOL_WIDTH ** -0.5)
    inp['w_branch_mla'] = nrm((L, MLA_HEADS * MLA_V, D), (MLA_HEADS * MLA_V) ** -0.5)
    inp['w_branch_gla'] = nrm((L, GLA_HEADS * GLA_DV, D), (GLA_HEADS * GLA_DV) ** -0.5)
    inp['w_out'] = nrm((L, D, D), BETA * D ** -0.5)
    inp['mem_w_q'] = nrm((L, D, D), D ** -0.5)
    inp['mem_w_k'] = nrm((L, D, D), D ** -0.5)
    inp['mem_w_v'] = nrm((L, D, D), D ** -0.5)
    inp['mem_w_o'] = nrm((L, D, D), BETA * D ** -0.5)
    inp['w_ffn2_in'] = nrm((L, D, 2 * D_FF), D ** -0.5)
    inp['w_ffn2_out'] = nrm((L, D_FF, D), BETA * D_FF ** -0.5)
    return inp

def reference(x_prompt, x_sample, mem_prompt, cache_pool, cache_mla_ckv, cache_mla_krope, state_gla,
              cache_mem_k, cache_mem_v, ln_g, ln_b, w_ffn1_in, w_ffn1_out, w_in, pool_w, pool_scale,
              mla_q_norm, mla_kv_norm, mla_w_uq, mla_w_uk, mla_w_uv, gla_w_a2, gla_b_a, gla_norm,
              w_branch_pool, w_branch_mla, w_branch_gla, w_out, mem_w_q, mem_w_k, mem_w_v, mem_w_o,
              w_ffn2_in, w_ffn2_out):
    B = x_prompt.shape[0]
    past_len = cache_mla_ckv.shape[2]
    pool_hist0 = jnp.zeros((B, POOL_HIST, POOL_WIDTH), x_prompt.dtype)
    gla0 = jnp.zeros((B, GLA_HEADS, GLA_DK, GLA_DV), jnp.float32)
    xp, xs = x_prompt, x_sample
    pool_p, pool_s, ckv_p, ckv_s, kr_p, kr_s, gla_p, gla_s, mk_list, mv_list = ([] for _ in range(10))
    for l in range(DEPTH):
        lw = {'ln_g': ln_g[l], 'ln_b': ln_b[l], 'w_ffn1_in': w_ffn1_in[l], 'w_ffn1_out': w_ffn1_out[l],
              'w_in': w_in[l], 'pool_w': pool_w[l], 'pool_scale': pool_scale[l],
              'mla_q_norm': mla_q_norm[l], 'mla_kv_norm': mla_kv_norm[l], 'mla_w_uq': mla_w_uq[l],
              'mla_w_uk': mla_w_uk[l], 'mla_w_uv': mla_w_uv[l], 'gla_w_a2': gla_w_a2[l],
              'gla_b_a': gla_b_a[l], 'gla_norm': gla_norm[l], 'w_branch_pool': w_branch_pool[l],
              'w_branch_mla': w_branch_mla[l], 'w_branch_gla': w_branch_gla[l], 'w_out': w_out[l],
              'mem_w_q': mem_w_q[l], 'mem_w_o': mem_w_o[l],
              'w_ffn2_in': w_ffn2_in[l], 'w_ffn2_out': w_ffn2_out[l]}
        mk, mv = memory_kv(mem_prompt, mem_w_k[l], mem_w_v[l])
        xp, np_, nc_, nk_, ng_ = trunk_layer(xp, 0, pool_hist0, gla0, None, None, mk, mv, lw)
        pool_p.append(np_); ckv_p.append(nc_); kr_p.append(nk_); gla_p.append(ng_)
        mk_list.append(mk); mv_list.append(mv)
        xs, ns_, cs_, ks_, gs_ = trunk_layer(xs, past_len, cache_pool[l], state_gla[l], cache_mla_ckv[l],
                                             cache_mla_krope[l], cache_mem_k[l], cache_mem_v[l], lw)
        pool_s.append(ns_); ckv_s.append(cs_); kr_s.append(ks_); gla_s.append(gs_)
    return (xp, xs,
            jnp.stack(pool_p, 0), jnp.stack(pool_s, 0),
            jnp.stack(ckv_p, 0), jnp.stack(ckv_s, 0),
            jnp.stack(kr_p, 0), jnp.stack(kr_s, 0),
            jnp.stack(gla_p, 0), jnp.stack(gla_s, 0),
            jnp.stack(mk_list, 0), jnp.stack(mv_list, 0))


_drawn_inputs = setup_inputs


def setup_inputs(seed=0):
    import zlib

    import numpy as np

    out = dict(_drawn_inputs(seed))
    spreads = {}
    factors = {'cache_mla_krope': 3.511,
     'pool_scale': 8.0,
     'mla_q_norm': 8.0,
     'mla_kv_norm': 2.97,
     'gla_norm': 8.0}
    for name, (base, spread) in spreads.items():
        noise = np.random.default_rng([zlib.crc32(name.encode()), seed]).standard_normal(out[name].shape)
        drawn = base * np.exp(spread * noise) if base else spread * noise
        out[name] = __import__('jax').numpy.asarray(drawn.astype(out[name].dtype))
    for name, factor in factors.items():
        out[name] = (out[name] * factor).astype(out[name].dtype)
    return out
```

```python
from contextlib import ExitStack

import numpy as np

import concourse.bass as bass
from concourse import mybir

F32 = mybir.dt.float32
F32R = mybir.dt.float32r
U8 = mybir.dt.uint8
ALU = mybir.AluOpType
ACT = mybir.ActivationFunctionType
AX = mybir.AxisListType

D = 1024
KC = D // 128
NP_, NS = 512, 32
T = NP_ + NS
TH = T // 2
PAST = 128
NMEM = 256
L = 2
DFF = 2816
FC = DFF // 128
PAD = 96
EPS = 1e-5
ALPHA = (2 * L) ** 0.25
HIST = 15
MLA_SCALE = (64 + 32) ** -0.5
MEM_SCALE = 256 ** -0.5
NK = T + PAST
KH = NK // 2
LEVELS = (64, 32, 16, 8, 4, 2, 1)

PHASES = [("f1i", 22, 8), ("f1o", 8, 11), ("win", 6, 8), ("gv", 1, 8),
          ("vup", 1, 4), ("mla", 2, 6), ("br", 16, 8), ("wo", 4, 8), ("memk", 4, 8), ("memv", 4, 8),
          ("cq", 4, 8), ("co", 4, 8),
          ("f2i", 22, 8), ("f2o", 8, 11)]
PAIRS = {n: p for n, p, _ in PHASES}
TILES = {n: t for n, _, t in PHASES}
BASE = {}
for _n, _p, _ in PHASES:
    BASE[_n] = sum(PAIRS[m] for m in BASE)
NEXT = {a[0]: b[0] for a, b in zip(PHASES, PHASES[1:] + PHASES[:1])}
PAIRS_L = sum(PAIRS.values())
USES = [("f1i", 22), ("f1o", 4), ("win", 6), ("br", 16), ("wo", 4), ("memk", 4), ("memv", 2), ("cq", 4),
        ("co", 4), ("f2i", 22), ("f2o", 4)]
UBASE = {}
_t = 0
for _n, _u in USES:
    UBASE[_n] = _t
    _t += _u
USES_L = _t
SM_LNG, SM_LNB, SM_PS, SM_QN, SM_KN, SM_BA, SM_GN, SM_PW, SM_WA = 0, 32, 64, 66, 68, 70, 71, 72, 328
SM_W = 456


def build(nc, io):
    with ExitStack() as ctx:
        at = [(nc.sbuf_base + 31) // 32 * 32]

        def place(name, cols, dt=F32, size=4):
            t = nc.alloc_sbuf_tensor_at(name, [128, cols], dt, offset=at[0])
            at[0] += (cols * size + 31) // 32 * 32
            return t

        def sem(name):
            return ctx.enter_context(nc.semaphore(name))

        XH = place("XH", KC * T + PAD, F32R)
        XL = place("XL", KC * T + PAD, F32R)
        Yf = place("Y", KC * T)
        Y = Yf[:, :].rearrange("p (c t) -> p c t", c=KC)
        WR = [place(f"WR{s}", 11 * 128) for s in (0, 1)]
        WH = [place(f"WH{s}", 11 * 128, F32R) for s in (0, 1)]
        WL = [place(f"WL{s}", 11 * 128, F32R) for s in (0, 1)]
        SMALL = place("SMALL", SM_W)
        TAB = place("TAB", 4 * T)
        QTAB, KCOS, KSIN, RESET = (TAB[:, i * T:(i + 1) * T] for i in range(4))
        CST = place("CST", 3 * 128 + 34)
        IDENT, ONES, BLK = (CST[:, i * 128:(i + 1) * 128] for i in range(3))
        INVC = CST[:, 384:416].rearrange("p (c t) -> p c t", c=2)
        INVW = CST[:, 416:418]
        MASK = place("MASK", 8 * 128, U8, 1)
        SC = place("SC", 32)
        LN_ = place("LNT", 6 * T)
        LNT = [LN_[:, i * T:(i + 1) * T] for i in range(6)]
        KT = [LN_[:, 2 * T + e * NK:2 * T + (e + 1) * NK] for e in (0, 1)]
        YS, QS, MEAN, RSTD = LNT[0], LNT[1], LNT[2], LNT[3]
        SQ = LNT[4:6]
        UW = 2 * HIST + T
        UQ = HIST + NP_
        W0 = at[0]

        HH = place("HH", FC * T, F32R)
        HL = place("HL", FC * T, F32R)
        end = at[0]
        at[0] = W0
        BH = place("BH", KC * T, F32R)
        BL = place("BL", KC * T, F32R)
        R0 = at[0]
        QL = place("QL", 2 * T)
        CK = place("CK", 2 * NK)
        KR = place("KR", NK)
        R1 = at[0]
        GA = place("GA", T)
        GQ = place("GQ", T)
        GK = place("GK", T)
        SG = place("SG", 2 * T)
        VT = place("VT", 5 * 256)
        U = place("U", 2 * (2 * HIST + T))
        KDT = place("KDT", 5 * 128)
        SB = place("SB", 6 * 256)
        A = place("A", 4 * NP_)
        AS = place("AS", 4 * NS)
        O = place("O", 2 * T)
        assert at[0] <= end
        at[0] = R1
        QH = place("QH", 2 * T, F32R)
        QO = place("QO", 2 * T, F32R)
        CH = place("CH", 2 * NK + PAD, F32R)
        CO = place("CO", 2 * NK + PAD, F32R)
        V = place("V", 6 * 512)
        PW = 1280 + 160
        P1 = place("P1", PW)
        PT = place("PT", 1280 + 64)
        assert at[0] <= end
        P0 = nc.alloc_sbuf_tensor_at("P0", [128, PW], F32, offset=R0)
        P = [P0, P1]
        at[0] = R0
        MXH = place("MXH", KC * T, F32R)
        MXL = place("MXL", KC * T, F32R)
        MRAW = place("MRAW", KC * NMEM)
        MMH = place("MMH", KC * NMEM, F32R)
        MML = place("MML", KC * NMEM, F32R)
        assert at[0] <= end
        at[0] = W0
        MK = [place("MKp", KC * NMEM), place("MKs", KC * NMEM)]
        MV = [place("MVp", 2 * D), place("MVs", 2 * D)]
        CP = [place("CP0", 1280), place("CP1", 1280)]
        CPT = place("CPT", 2 * T)
        OH = place("OH", KC * T, F32R)
        OL = place("OL", KC * T, F32R)
        assert at[0] <= end

        PS = ctx.enter_context(nc.psum_tensor("PS", [128, 8, 512], F32))

        def banks2(b, n=TH):
            return PS[:, b:b + 2, 0:n]

        def two(ap):
            return ap.rearrange("p (h t) -> p h t", h=2)

        CPV = [((0, 7), 1)] * 3 + [((5, 7), 6)]

        landed = [sem(f"w_landed{s}") for s in (0, 1)]
        hi_ready = [sem(f"w_hi{s}") for s in (0, 1)]
        lo_ready = [sem(f"w_lo{s}") for s in (0, 1)]
        w_used = [sem(f"w_used{s}") for s in (0, 1)]
        bank_free = [sem(f"bank_free{s}") for s in (0, 1)]
        names = ("const_in small_in x_in0 x_in1 x_in2 x_in3 x_hi x_ready x_done mem_in mem_hi mem_ready memk_out memv_out mem_st "
                 "silu h_ready y_upd y_sq q_add stats_ready stats_mm mean msq var rstd ln_d "
                 "hist_in caches_in gla_in u_ready pool_done pool_s pooled pool_mm pool_hi pool_lo kr_ready "
                 "rq_sq rq_mm rq_v rq_r ck_in latr_hi lat_ready tanh_r sg_done gv_mm vt_ready z_in z_mm z_abs z_l la_ok B_ok eb_ok kdE kd_sub kd_ok "
                 "kdt_mm kdt_ok ds_mm sb_ok lv_e lv_x lv_E lv_mm lv_sel o_mm o_ok o_sq o_ms o_v o_r o_y o_hi o_lo "
                 "v_mm v_ok krt qk_ok sc_mm mx_ok exp_ok p_ok pt_mm pt_a pt_d pv_mm pv_hi pv_lo "
                 "ta_ok m_ok mx_hi mx_lo tf_free br_rd "
                 "cmem_in cq_ok csc_mm cmx_ok cexp_ok cp_ok cpt_mm cpt_d cpv_mm cpv_hi cpv_lo "
                 "st_pool st_ck st_kr st_gla st_mem st_y waited").split()
        S = {n: sem(n) for n in names}

        def settle(eng):
            eng.sem_inc(S["waited"], 1)
        block = ctx.enter_context(nc.Block())

        @block.sync
        def _(sp):
            with sp.Fori(0, L) as l:
                for name, pairs, tiles in PHASES:
                    with sp.Fori(0, pairs) as p:
                        c = l * PAIRS_L + BASE[name] + p
                        for s in (0, 1):
                            sp.wait_ge(lo_ready[s], c + 1)
                            sp.dma_start(WR[s][:, 0:tiles * 128], io[name][l, p * 2 + s]).then_inc(landed[s], 16)
            for s in (0, 1):
                sp.wait_ge(lo_ready[s], L * PAIRS_L + 1)
                sp.dma_start(WR[s][:, 0:TILES["f1i"] * 128], io["f1i"][0, s]).then_inc(landed[s], 16)

        @block.gpsimd
        def _(pool):
            for s in (0, 1):
                pool.sem_inc(lo_ready[s], 1)

            def lo(s, tiles, c):
                pool.wait_ge(hi_ready[s], c + 1)
                n = tiles * 128
                pool.tensor_tensor(WL[s][:, 0:n], WR[s][:, 0:n], WH[s][:, 0:n].bitcast(F32),
                                   ALU.subtract).then_inc(lo_ready[s], 1)

            def phase(l, name):
                n = PAIRS[name]
                base = l * PAIRS_L + BASE[name]
                if n > 1:
                    with pool.Fori(0, n - 1) as p:
                        for s in (0, 1):
                            lo(s, TILES[name], base + p + 1)
                for s in (0, 1):
                    lo(s, TILES[NEXT[name]], base + n)

            def x_lo_chunk(count, c):
                pool.wait_ge(S["x_hi"], count * KC + c + 1)
                xs = bass.ds(c * T, T)
                pool.tensor_tensor(XL[:, xs], Yf[:, xs], XH[:, xs].bitcast(F32),
                                   ALU.subtract).then_inc(S["x_ready"], 1)

            def x_lo(count):
                with pool.Fori(0, KC) as c:
                    x_lo_chunk(count, c)

            for s in (0, 1):
                lo(s, TILES["f1i"], 0)
            x_lo(0)
            with pool.Fori(0, L) as l:
                for name in ("f1i", "f1o"):
                    phase(l, name)
                x_lo(4 * l + 1)
                for name in ("win", "gv", "vup", "mla", "br", "wo"):
                    phase(l, name)
                for i, (name, p) in enumerate([(n, p) for n in ("memk", "memv") for p in range(4)]):
                    for s in (0, 1):
                        lo(s, TILES["memk"], l * PAIRS_L + BASE[name] + p + 1)
                    if 1 <= i < 5:
                        for c in (2 * i - 2, 2 * i - 1):
                            x_lo_chunk(4 * l + 2, c)
                for name in ("cq", "co"):
                    phase(l, name)
                x_lo(4 * l + 3)
                phase(l, "f2i")
                phase(l, "f2o")
                x_lo(4 * l + 4)

        @block.tensor
        def _(pe):
            for s in (0, 1):
                pe.sem_inc(w_used[s], 1)

            def mm(out, lhsT, rhs, start, stop):
                return pe.matmul(out, lhsT, rhs, start=start, stop=stop, skip_group_check=True)

            def gemm(s, c, tiles, start=True, stop=True):
                pe.wait_ge(hi_ready[s], c + 1)
                for i, outs, first, last in tiles:
                    w = WH[s][:, i * 128:(i + 1) * 128]
                    for out, xh, xl in outs:
                        mm(out, w, xh, start and first, False)
                    for out, xh, xl in outs:
                        mm(out, w, xl, False, False)
                pe.wait_ge(lo_ready[s], c + 2)
                for i, outs, first, last in tiles:
                    w = WL[s][:, i * 128:(i + 1) * 128]
                    for out, xh, xl in outs:
                        m = mm(out, w, xh, False, stop and last)
                m.then_inc(w_used[s], 1)

            def halves(b, H, Lo, k, n=TH, width=T):
                return [(PS[:, b + h, 0:n], H[:, k * width + h * n:k * width + (h + 1) * n],
                         Lo[:, k * width + h * n:k * width + (h + 1) * n]) for h in (0, 1)]

            def chunk_tiles(b, H, Lo, ks=range(KC)):
                ks = list(ks)
                return [(i, halves(b, H, Lo, k), i == 0, i == len(ks) - 1) for i, k in enumerate(ks)]

            def first_pair(l, name, n, ready="x_ready", H=XH, Lo=XL):
                c = l * PAIRS_L + BASE[name]
                for s in (0, 1):
                    pe.wait_ge(bank_free[s], l * USES_L + UBASE[name] + 1)
                    pe.wait_ge(lo_ready[s], c + 2)
                for k in range(KC):
                    pe.wait_ge(S[ready], n * KC + k + 1)
                    for s in (0, 1):
                        wh, wl = (W[s][:, k * 128:(k + 1) * 128] for W in (WH, WL))
                        outs = halves(2 * s, H, Lo, k)
                        for out, xh, xl in outs:
                            mm(out, wh, xh, k == 0, False)
                        for out, xh, xl in outs:
                            mm(out, wh, xl, False, False)
                        for out, xh, xl in outs:
                            m = mm(out, wl, xh, False, k == KC - 1)
                        if k == KC - 1:
                            m.then_inc(w_used[s], 1)

            def standard(l, name, H, Lo, start=0):
                with pe.Fori(start, PAIRS[name]) as p:
                    for s in (0, 1):
                        pe.wait_ge(bank_free[s], l * USES_L + UBASE[name] + p + 1)
                        gemm(s, l * PAIRS_L + BASE[name] + p, chunk_tiles(2 * s, H, Lo))

            def ffn_out(l, name, n):
                pe.wait_ge(S["h_ready"], n * FC + 11)
                settle(pe)
                with pe.Fori(0, PAIRS[name] // 2) as q:
                    for u in (0, 1):
                        pe.wait_ge(bank_free[u], l * USES_L + UBASE[name] + q + 1)
                        for s in (0, 1):
                            c = l * PAIRS_L + BASE[name] + q * 2 + u
                            ks = range(11 * s, 11 * s + 11)
                            if s:
                                pe.wait_ge(S["h_ready"], (n + 1) * FC)
                            gemm(s, c, chunk_tiles(2 * u, HH, HL, ks), start=s == 0, stop=s == 1)

            def ln_stats(l, j):
                pe.wait_ge(S["stats_ready"], l * 4 + j + 1)
                for b, src in ((4, YS), (6, QS)):
                    for h in (0, 1):
                        m = mm(PS[:, b + h, 0:TH], ONES, src[:, h * TH:(h + 1) * TH], True, True)
                m.then_inc(S["stats_mm"], 1)

            def rms_stats(b, sq):
                for h in (0, 1):
                    for c in (0, 1):
                        m = mm(PS[:, b + h, 0:TH], ONES, sq[:, c * T + h * TH:c * T + (h + 1) * TH], c == 0, c == 1)
                return m

            pe.wait_ge(S["const_in"], 16 * 3)
            with pe.Fori(0, L) as l:
                first_pair(l, "f1i", 4 * l)
                standard(l, "f1i", XH, XL, 1)
                ffn_out(l, "f1o", l * 2 + 0)
                ln_stats(l, 0)

                first_pair(l, "win", 4 * l + 1)
                standard(l, "win", XH, XL, 1)
                cgv = l * PAIRS_L + BASE["gv"]
                for s in (0, 1):
                    for part, W, ready in ((0, WH, hi_ready), (1, WL, lo_ready)):
                        pe.wait_ge(ready[s], cgv + 1 + part)
                        for kk in range(4):
                            k = 4 * s + kk
                            w = W[s][:, kk * 256:(kk + 1) * 256]
                            for t in range(5):
                                out = PS[:, 4 + t // 2, (t % 2) * 256:(t % 2 + 1) * 256]
                                o = k * T + t * 128
                                m = mm(out, XH[:, o:o + 128], w, k == 0 and part == 0 and t % 2 == 0,
                                       k == 7 and part == 1)
                                if part == 0:
                                    m = mm(out, XL[:, o:o + 128], w, False, False)
                    m.then_inc(w_used[s], 1)

                pe.wait_ge(S["pooled"], l + 1)
                for s in (0, 1):
                    pe.wait_ge(bank_free[s], l * USES_L + UBASE["win"] + 7)
                for c in (0, 1):
                    for h in (0, 1):
                        m = mm(PS[:, 2 * c + h, 0:TH], SMALL[:, SM_PW + c * 128:SM_PW + (c + 1) * 128],
                               O[:, c * T + h * TH:c * T + (h + 1) * TH], True, True)
                m.then_inc(S["pool_mm"], 1)
                pe.wait_ge(S["vt_ready"], l + 1)
                for h in (0, 1):
                    m = mm(PS[:, 4 + h, 0:TH], SMALL[0:16, SM_WA:SM_WA + 128], GA[0:16, h * TH:(h + 1) * TH], True, True)
                m.then_inc(S["z_mm"], 1)
                pe.wait_ge(S["rq_sq"], l * 2 + 1)
                rms_stats(6, LN_[:, 0:2 * T]).then_inc(S["rq_mm"], 1)
                pe.wait_ge(S["rq_v"], l * 2 + 1)
                pe.wait_ge(S["rq_sq"], l * 2 + 2)
                rms_stats(6, LN_[:, 0:2 * T]).then_inc(S["rq_mm"], 1)

                pe.wait_ge(S["kd_ok"], l + 1)
                pe.wait_ge(S["pool_lo"], l + 1)
                for i in range(5):
                    n = 128 if i < 4 else NS
                    m = pe.transpose(PS[0:n, i, 0:128], LNT[3][:, i * 128:i * 128 + n], IDENT)
                m.then_inc(S["kdt_mm"], 1)
                pe.wait_ge(S["kdt_ok"], l + 1)
                for i in range(5):
                    n = 128 if i < 4 else NS
                    m = mm(PS[:, i, 0:256], KDT[0:n, i * 128:(i + 1) * 128], VT[0:n, i * 256:(i + 1) * 256], True, True)
                m.then_inc(S["ds_mm"], 1)
                pe.wait_ge(S["sb_ok"], l + 1)
                for j in range(8):
                    if j < 7:
                        pe.wait_ge(S["lv_x"], l * 7 + j + 1)
                    pe.wait_ge(S["lv_sel"], l * 8 + j + 1)
                    a, b = (LNT[5], LNT[5]) if j < 7 else (GK, GQ)
                    for i in range(4):
                        for h in range(4):
                            r = slice(32 * h, 32 * h + 32)
                            m = mm(PS[:, 4 + h, i * 128:(i + 1) * 128], a[r, i * 128:(i + 1) * 128],
                                   b[r, i * 128:(i + 1) * 128], True, True)
                    if j >= 2:
                        for h in range(4):
                            r = slice(32 * h, 32 * h + 32)
                            m = mm(PS[0:NS, h, 0:NS], a[r, NP_:T], b[r, NP_:T], True, True)
                    m.then_inc(S["lv_mm"], 1)
                pe.wait_ge(S["lv_sel"], l * 8 + 9)
                for g in (0, 1):
                    for i in range(5):
                        n = 128 if i < 4 else NS
                        bank, o = (4 + g, i * 128) if i < 4 else (6 + g, 0)
                        sb = i - 1 if i < 4 else 4
                        if i > 0:
                            mm(PS[:, bank, o:o + n], SB[:, sb * 256 + g * 128:sb * 256 + (g + 1) * 128],
                               LNT[2][:, i * 128:i * 128 + n], True, False)
                        for e in (0, 1):
                            h = 2 * g + e
                            a = A[:, h * NP_ + i * 128:h * NP_ + (i + 1) * 128] if i < 4 else AS[0:NS, h * NS:(h + 1) * NS]
                            m = mm(PS[64 * e:64 * e + 64, bank, o:o + n], VT[0:n, i * 256 + h * 64:i * 256 + (h + 1) * 64],
                                   a, i == 0, True)
                m.then_inc(S["o_mm"], 1)
                pe.wait_ge(S["o_sq"], l + 1)
                for g in (0, 1):
                    for h in (0, 1):
                        m = mm(PS[:, 2 * g + h, 0:TH], BLK, LN_[:, g * T + h * TH:g * T + (h + 1) * TH], True, True)
                m.then_inc(S["o_ms"], 1)

                pe.wait_ge(S["lat_ready"], l + 1)
                pe.wait_ge(S["o_v"], l + 1)
                cv = l * PAIRS_L + BASE["vup"]
                for s in (0, 1):
                    for part, W, ready in ((0, WH, hi_ready), (1, WL, lo_ready)):
                        pe.wait_ge(ready[s], cv + 1 + part)
                        for t in range(6):
                            o = s * NK + t * 128
                            m = mm(PS[:, t, 0:512], CH[:, o:o + 128], W[s][:, 0:512], s == 0 and part == 0, s == 1 and part == 1)
                            if part == 0:
                                m = mm(PS[:, t, 0:512], CO[:, o:o + 128], W[s][:, 0:512], False, False)
                    m.then_inc(w_used[s], 1)
                pe.wait_ge(S["v_ok"], l * 2 + 2)
                for hp in range(4):
                    s = hp % 2
                    c = l * PAIRS_L + BASE["mla"] + hp // 2
                    if hp:
                        pe.wait_ge(S["pv_lo"], l * 4 + hp)
                    gemm(s, c, [(2 * e + k, halves(2 * e, QH, QO, k), k == 0, k == 1) for e in (0, 1) for k in (0, 1)]
                         + [(4 + k, halves(4, CH, CO, k, KH, NK), k == 0, k == 1) for k in (0, 1)])
                    pe.wait_ge(S["qk_ok"], l * 8 + 2 * hp + 2)
                    for e in (0, 1):
                        q, kt = LNT[e], KT[e]
                        for i, bank, o in ((3, 0, 0), (2, 1, 0), (0, 1, 384), (1, 2, 0)):
                            n = 128 * (i + 1)
                            mm(PS[:, 3 * e + bank, o:o + n], q[:, i * 128:(i + 1) * 128], kt[:, 0:n], True, True)
                        mm(PS[0:NS, 3 * e + 2, 256:416], q[:, NP_:T], kt[:, NP_:NK], True, True).then_inc(S["sc_mm"], 1)
                    for e in (0, 1):
                        h = 2 * hp + e
                        pe.wait_ge(S["p_ok"], l * 8 + h + 1)
                        if e:
                            pe.wait_ge(S["pt_a"], l * 8 + h)
                            pe.wait_ge(S["pt_d"], l * 8 + h)
                        p = P[e]
                        for kb in range(4):
                            for i in range(kb, 4):
                                bank, o = ((6, 0), (7, 0), (3 * e, 0), (7, 384))[kb]
                                po = 128 * (i * (i + 1) // 2 + kb)
                                pe.transpose(PS[:, bank, o + (i - kb) * 128:o + (i - kb + 1) * 128], p[:, po:po + 128], IDENT)
                        pe.transpose(PS[:, 3 * e, 256:288], p[0:NS, 1280:1408], IDENT[0:NS, 0:NS])
                        pe.transpose(PS[0:NS, 3 * e, 288:320], p[0:NS, 1408:1440], IDENT[0:NS, 0:NS]).then_inc(S["pt_mm"], 1)
                        pe.wait_ge(S["pt_a"], l * 8 + h + 1)
                        pe.wait_ge(S["pt_d"], l * 8 + h + 1)
                        r = slice(64 * e, 64 * e + 64)
                        for kb in range(4):
                            po = (0, 512, 896, 1152)[kb]
                            mm(PS[r, 1, kb * 128:512], V[:, kb * 512 + h * 64:kb * 512 + (h + 1) * 64],
                               PT[:, po:po + 512 - 128 * kb], kb == 0, kb == 3)
                        mm(PS[r, 2, 0:NS], V[:, 4 * 512 + h * 64:4 * 512 + (h + 1) * 64], PT[:, 1280:1312], True, False)
                        mm(PS[r, 2, 0:NS], V[0:NS, 5 * 512 + h * 64:5 * 512 + (h + 1) * 64], PT[0:NS, 1312:1344],
                           False, True).then_inc(S["pv_mm"], 1)

                pe.wait_ge(S["pv_lo"], l * 4 + 4)
                settle(pe)
                with pe.Fori(0, KC) as m_:
                    for g in range(4):
                        s = g % 2
                        c = l * PAIRS_L + BASE["br"] + m_ * 2 + g // 2
                        pe.wait_ge(bank_free[s], l * USES_L + UBASE["br"] + m_ * 2 + g // 2 + 1)
                        if g < 3:
                            gemm(s, c, chunk_tiles(2 * s, XH, XL))
                        else:
                            pe.wait_ge(S["br_rd"], l * KC + m_ + 1)
                            gemm(s, c, [(k, halves(b, BH, BL, k), k == k0, k == k1 - 1)
                                        for b, k0, k1 in ((4, 0, 2), (6, 2, 6), (2, 6, 8)) for k in range(k0, k1)])
                first_pair(l, "wo", l, "mx_lo", MXH, MXL)
                standard(l, "wo", MXH, MXL, 1)
                ln_stats(l, 1)

                pe.wait_ge(S["mem_ready"], l + 1)
                settle(pe)
                with pe.Fori(0, PAIRS["memk"]) as p:
                    for s in (0, 1):
                        pe.wait_ge(bank_free[s], l * USES_L + UBASE["memk"] + p + 1)
                        gemm(s, l * PAIRS_L + BASE["memk"] + p,
                             [(k, [(PS[:, 2 * s, 0:NMEM], MMH[:, k * NMEM:(k + 1) * NMEM],
                                    MML[:, k * NMEM:(k + 1) * NMEM])], k == 0, k == KC - 1) for k in range(KC)])
                with pe.Fori(0, 2) as q:
                    for u in (0, 1):
                        pe.wait_ge(bank_free[u], l * USES_L + UBASE["memv"] + q + 1)
                        for s in (0, 1):
                            c = l * PAIRS_L + BASE["memv"] + q * 2 + u
                            kk0 = 4 * s
                            pe.wait_ge(hi_ready[s], c + 1)
                            for kk in range(4):
                                w = WH[s][:, kk * 256:(kk + 1) * 256]
                                for t in (0, 1):
                                    o = (kk0 + kk) * NMEM + t * 128
                                    out = PS[:, 2 * u, t * 256:(t + 1) * 256]
                                    mm(out, MMH[:, o:o + 128], w, kk0 + kk == 0 and t == 0, False)
                                    mm(out, MML[:, o:o + 128], w, False, False)
                            pe.wait_ge(lo_ready[s], c + 2)
                            for kk in range(4):
                                w = WL[s][:, kk * 256:(kk + 1) * 256]
                                for t in (0, 1):
                                    o = (kk0 + kk) * NMEM + t * 128
                                    out = PS[:, 2 * u, t * 256:(t + 1) * 256]
                                    m = mm(out, MMH[:, o:o + 128], w, False, kk0 + kk == 7)
                            m.then_inc(w_used[s], 1)

                pe.wait_ge(S["cmem_in"], (l + 1) * 32)
                first_pair(l, "cq", 4 * l + 2)
                free = l * USES_L + UBASE["cq"]
                for h in range(4):
                    for s in (0, 1):
                        pe.wait_ge(bank_free[s], free + h + 2)
                    for i in range(4):
                        for c in (0, 1):
                            mm(PS[:, 4 + i // 2, (i % 2) * 256:(i % 2 + 1) * 256], LNT[c][:, i * 128:(i + 1) * 128],
                               MK[0][:, (2 * h + c) * NMEM:(2 * h + c + 1) * NMEM], c == 0, c == 1)
                    for c in (0, 1):
                        m = mm(PS[0:NS, 6, 0:NMEM], LNT[c][:, NP_:T], MK[1][:, (2 * h + c) * NMEM:(2 * h + c + 1) * NMEM],
                               c == 0, c == 1)
                    m.then_inc(S["csc_mm"], 1)
                    if h:
                        pe.wait_ge(S["cpv_lo"], l * 8 + 2 * h)
                    if h < 3:
                        gemm(0, l * PAIRS_L + BASE["cq"] + h + 1, chunk_tiles(0, XH, XL))
                    pe.wait_ge(S["cp_ok"], l * 4 + h + 1)
                    p = CP[h % 2]
                    for kb in (0, 1):
                        for i in range(4):
                            pe.transpose(PS[:, (7, 4)[kb], i * 128:(i + 1) * 128],
                                         p[:, i * 256 + kb * 128:i * 256 + (kb + 1) * 128], IDENT)
                    for kb in (0, 1):
                        m = pe.transpose(PS[:, 6, kb * NS:(kb + 1) * NS], p[0:NS, 1024 + kb * 128:1024 + (kb + 1) * 128],
                                         IDENT[0:NS, 0:NS])
                    m.then_inc(S["cpt_mm"], 1)
                    if h < 3:
                        gemm(1, l * PAIRS_L + BASE["cq"] + h + 1, chunk_tiles(2, XH, XL))
                        pe.wait_ge(bank_free[0], free + h + 3)
                    pe.wait_ge(S["cpt_d"], l * 4 + h + 1)
                    bp, bs = CPV[h]
                    for c in (0, 1):
                        d0 = h * 256 + c * 128
                        for kb in (0, 1):
                            mm(PS[:, bs, c * NS:(c + 1) * NS], MV[1][:, kb * D + d0:kb * D + d0 + 128],
                               CPT[:, kb * T + NP_:(kb + 1) * T], kb == 0, kb == 1)
                    for c in (0, 1):
                        d0 = h * 256 + c * 128
                        for kb in (0, 1):
                            m = mm(PS[:, bp[c], 0:NP_], MV[0][:, kb * D + d0:kb * D + d0 + 128],
                                   CPT[:, kb * T:kb * T + NP_], kb == 0, kb == 1)
                        m.then_inc(S["cpv_mm"], 1)
                first_pair(l, "co", l, "cpv_lo", OH, OL)
                standard(l, "co", OH, OL, 1)
                ln_stats(l, 2)

                first_pair(l, "f2i", 4 * l + 3)
                standard(l, "f2i", XH, XL, 1)
                ffn_out(l, "f2o", l * 2 + 1)
                ln_stats(l, 3)

        @block.scalar
        def _(act):
            def f(out, in_, func, **kw):
                return act.activation(out, in_, func, **kw)

            def load(dst, src, s):
                return act.dma_start(dst, src).then_inc(S[s], 16)

            def convert(s, tiles, c):
                act.wait_ge(landed[s], (c + 1) * 16)
                act.wait_ge(w_used[s], c + 1)
                n = tiles * 128
                f(WH[s][:, 0:n], WR[s][:, 0:n], ACT.Copy).then_inc(hi_ready[s], 1)

            def pair(l, name, p, s, last):
                c = l * PAIRS_L + BASE[name] + p + 1
                if not last:
                    convert(s, TILES[name], c)
                else:
                    convert(s, TILES[NEXT[name]], c)

            def phase(l, name, body=None, unroll=1):
                n = PAIRS[name]
                if n > unroll:
                    with act.Fori(0, n // unroll - 1) as q:
                        for u in range(unroll):
                            for s in (0, 1):
                                pair(l, name, q * unroll + u, s, False)
                                if body:
                                    body(q * unroll + u, u, s, q)
                for u in range(unroll):
                    for s in (0, 1):
                        pair(l, name, n - unroll + u, s, u == unroll - 1)
                        if body:
                            body(n - unroll + u, u, s, n // unroll - 1)

            def square(n, m, b):
                act.wait_ge(S["y_upd"], n * KC + m + 1)
                act.wait_ge(S["q_add"], n * KC + m + 1)
                f(SQ[b], Yf[:, bass.ds(m * T, T)], ACT.Square).then_inc(S["y_sq"], 1)

            def ln_mean(n):
                act.wait_ge(S["stats_mm"], n + 1)
                f(two(MEAN), banks2(4), ACT.Copy, scale=1.0 / D).then_inc(S["mean"], 1)

            def ln_rstd(n):
                act.wait_ge(S["var"], n + 1)
                f(RSTD, RSTD, ACT.Ln)
                act.drain()
                f(RSTD, RSTD, ACT.Exp, scale=-0.5).then_inc(S["rstd"], 1)

            def ln_chunk(n, j, c):
                act.wait_ge(S["ln_d"], n * KC + c + 1)
                f(Y[:, c, :], Y[:, c, :], ACT.Identity, scale=SMALL[:, SM_LNG + j * KC + c:SM_LNG + j * KC + c + 1],
                  bias=SMALL[:, SM_LNB + j * KC + c:SM_LNB + j * KC + c + 1])
                act.drain()
                f(XH[:, c * T:(c + 1) * T], Y[:, c, :], ACT.Copy).then_inc(S["x_hi"], 1)

            def layer_norm(n, j):
                ln_mean(n)
                ln_rstd(n)
                for c in range(KC):
                    ln_chunk(n, j, c)

            for i in range(4):
                part = slice(i * 2 * T, (i + 1) * 2 * T)
                load(Yf[:, part], io["x"][:, part], f"x_in{i}")
            load(TAB[:, :], io["tab"], "const_in")
            load(CST[:, :], io["cst"], "const_in")
            load(LN_[:, 0:1024], io["mask"], "const_in")
            for s in (0, 1):
                convert(s, TILES["f1i"], 0)
            for c in range(KC):
                if c % 2 == 0:
                    act.wait_ge(S[f"x_in{c // 2}"], 16)
                f(XH[:, c * T:(c + 1) * T], Y[:, c, :], ACT.Copy).then_inc(S["x_hi"], 1)

            with act.Fori(0, L) as l:
                act.wait_ge(S["x_ready"], (4 * l + 1) * KC)
                load(SMALL[:, :], io["small"][l], "small_in")
                act.wait_ge(S["small_in"], (l + 1) * 16)

                def ffn_in(l, name):
                    def body(p, u, s, q):
                        if s == 0:
                            act.wait_ge(w_used[0], l * PAIRS_L + BASE[name] + p + 2)
                            act.wait_ge(bank_free[1], l * USES_L + UBASE[name] + p + 1)
                            f(two(LNT[2]), banks2(0), ACT.Silu).then_inc(bank_free[0], 1)
                    phase(l, name, body)

                def ffn_out(l, name, n):
                    phase(l, name, lambda p, u, s, q: square(n, p, u) if s else None, 2)

                ffn_in(l, "f1i")
                ffn_out(l, "f1o", 4 * l)
                act.wait_ge(S["stats_mm"], 4 * l + 1)
                for c in (0, 1):
                    load(U[:, c * UW + UQ:c * UW + UQ + HIST], io["pool_in"][l][:, c * HIST:(c + 1) * HIST], "hist_in")
                    load(CK[:, c * NK + T:(c + 1) * NK], io["ckv_in"][l][:, c * PAST:(c + 1) * PAST], "caches_in")
                for r in (64, 96):
                    load(KR[r:r + 32, T:NK], io["krope_in"][l], "caches_in")
                layer_norm(4 * l, 0)
                act.wait_ge(S["z_in"], l + 1)
                for h in range(4):
                    r = slice(32 * h, 32 * h + 32)
                    load(SB[r, 4 * 256 + h * 64:4 * 256 + (h + 1) * 64], io["gla_in"][l][r, :], "gla_in")

                def gr(p, u, s, q):
                    if isinstance(p, int):
                        act.wait_ge(w_used[s], l * PAIRS_L + BASE["win"] + p + 2)
                        f(two(LNT[s]), banks2(2 * s), ACT.Tanh, scale=0.5).then_inc(S["tanh_r"], 1)
                phase(l, "win", gr)
                phase(l, "gv")
                act.wait_ge(S["kr_ready"], l + 1)
                act.dma_start(io["krope"][l], KR[64:96, 0:T]).then_inc(S["st_kr"], 16)
                act.wait_ge(S["u_ready"], l + 1)
                for c in (0, 1):
                    act.dma_start(io["pool_p"][l][:, c * HIST:(c + 1) * HIST],
                                  U[:, c * UW + NP_:c * UW + NP_ + HIST]).then_inc(S["st_pool"], 16)
                    act.dma_start(io["pool_s"][l][:, c * HIST:(c + 1) * HIST],
                                  U[:, (c + 1) * UW - HIST:(c + 1) * UW]).then_inc(S["st_pool"], 16)
                act.wait_ge(S["pooled"], l + 1)
                for i, src in enumerate((QL, CK)):
                    if i:
                        act.wait_ge(S["rq_mm"], 2 * l + 1)
                        act.wait_ge(S["ck_in"], 2 * l + 1)
                    w = (T, NK)[i]
                    f(LN_[:, 0:2 * T].rearrange("p (c t) -> p c t", c=2),
                      src[:, :].rearrange("p (c t) -> p c t", c=2)[:, :, 0:T], ACT.Square).then_inc(S["rq_sq"], 1)
                    act.wait_ge(S["rq_v"], 2 * l + i + 1)
                    f(LNT[2], LNT[2], ACT.Ln)
                    act.drain()
                    f(LNT[2], LNT[2], ACT.Exp, scale=-0.5).then_inc(S["rq_r"], 1)
                act.wait_ge(S["pool_mm"], l + 1)
                for c in (0, 1):
                    f(two(BH[:, c * T:(c + 1) * T]), banks2(2 * c), ACT.Copy,
                      scale=SMALL[:, SM_PS + c:SM_PS + c + 1]).then_inc(S["pool_hi"], 1)
                act.wait_ge(S["ck_in"], 2 * l + 2)
                for c in (0, 1):
                    act.dma_start(io["ckv"][l][:, c * T:(c + 1) * T], CK[:, c * NK:c * NK + T]).then_inc(S["st_ck"], 16)
                act.wait_ge(S["z_mm"], l + 1)
                f(two(LNT[4]), banks2(4), ACT.Abs, bias=SMALL[:, SM_BA:SM_BA + 1]).then_inc(S["z_abs"], 1)
                act.drain()
                f(LNT[4], LNT[4], ACT.Exp, scale=-1.0)
                act.drain()
                f(LNT[4], LNT[4], ACT.Ln, bias=1.0).then_inc(S["z_l"], 1)
                act.wait_ge(S["B_ok"], l + 1)
                f(LNT[1], LNT[0], ACT.Exp, scale=1.0 / 16).then_inc(S["eb_ok"], 1)
                act.wait_ge(S["kd_sub"], l + 1)
                f(LNT[3], LNT[3], ACT.Exp, scale=1.0 / 16).then_inc(S["kdE"], 1)
                act.wait_ge(S["sb_ok"], l + 1)
                for h in range(4):
                    r = slice(32 * h, 32 * h + 32)
                    for sb, dst in ((3, "gla_p"), (5, "gla_s")):
                        act.dma_start(io[dst][l][r, :], SB[r, sb * 256 + h * 64:sb * 256 + (h + 1) * 64]).then_inc(S["st_gla"], 16)
                for j in range(7):
                    act.wait_ge(S["lv_e"], l * 7 + j + 1)
                    w = NP_ if j < 2 else T
                    f(LNT[4][:, 0:w], LNT[4][:, 0:w], ACT.Exp, scale=1.0 / 16).then_inc(S["lv_E"], 1)
                act.wait_ge(S["o_ok"], l + 1)
                f(LN_[:, 0:2 * T], O[:, :], ACT.Square).then_inc(S["o_sq"], 1)
                act.wait_ge(S["o_v"], l + 1)
                f(LN_[:, 2 * T:4 * T], LN_[:, 2 * T:4 * T], ACT.Ln)
                act.drain()
                f(LN_[:, 2 * T:4 * T], LN_[:, 2 * T:4 * T], ACT.Exp, scale=-0.5).then_inc(S["o_r"], 1)
                act.wait_ge(S["o_y"], l + 1)
                f(BH[:, 6 * T:8 * T], O[:, :], ACT.Copy).then_inc(S["o_hi"], 1)

                act.wait_ge(S["o_lo"], l + 1)
                act.wait_ge(S["st_pool"], (l + 1) * 64)
                act.wait_ge(S["st_gla"], (l + 1) * 128)
                act.wait_ge(S["st_ck"], (l + 1) * 32)
                act.wait_ge(S["caches_in"], (l + 1) * 64)
                f(QH[:, :], QL[:, :], ACT.Copy).then_inc(S["latr_hi"], 1)
                f(CH[:, 0:2 * NK], CK[:, :], ACT.Copy).then_inc(S["latr_hi"], 1)
                for s in (0, 1):
                    pair(l, "vup", 0, s, True)
                act.wait_ge(w_used[1], l * PAIRS_L + BASE["vup"] + 2)
                f(V[:, 4 * 512:5 * 512], PS[:, 4, 0:512], ACT.Copy)
                f(V[0:NS, 5 * 512:6 * 512], PS[0:NS, 5, 0:512], ACT.Copy).then_inc(S["v_ok"], 1)
                for hp in range(4):
                    s = hp % 2
                    act.wait_ge(w_used[s], l * PAIRS_L + BASE["mla"] + hp // 2 + 2)
                    for e in (0, 1):
                        i = f(two(KT[e][0:64, :]), PS[64 * e:64 * e + 64, 4:6, 0:KH], ACT.Copy)
                    i.then_inc(S["qk_ok"], 1)
                    pair(l, "mla", hp // 2, s, hp >= 2)
                    for e in (0, 1):
                        h = 2 * hp + e
                        act.wait_ge(S["mx_ok"], l * 8 + h + 1)
                        c0 = 16 * e
                        for i, bank, o in ((3, 0, 0), (2, 1, 0), (0, 1, 384), (1, 2, 0)):
                            for hf in (0, 1):
                                r = slice(64 * hf, 64 * hf + 64)
                                n = 128 * i + 64 * (hf + 1)
                                po = 128 * (i * (i + 1) // 2)
                                f(P[e][r, po:po + n], PS[r, 3 * e + bank, o:o + n], ACT.Exp, scale=MLA_SCALE,
                                  bias=SC[r, c0 + 5 + i:c0 + 6 + i], accum_out=SC[r, c0 + 10 + i:c0 + 11 + i])
                        f(P[e][0:NS, 1280:1440], PS[0:NS, 3 * e + 2, 256:416], ACT.Exp, scale=MLA_SCALE,
                          bias=SC[0:NS, c0 + 9:c0 + 10], accum_out=SC[0:NS, c0 + 14:c0 + 15])
                        act.drain().then_inc(S["exp_ok"], 1)
                    for e in (0, 1):
                        h = 2 * hp + e
                        act.wait_ge(S["pt_mm"], l * 8 + h + 1)
                        if e:
                            act.wait_ge(S["pv_mm"], l * 8 + h)
                        f(PT[:, 896:1152], PS[:, 3 * e, 0:256], ACT.Copy)
                        f(PT[:, 1280:1312], PS[:, 3 * e, 256:288], ACT.Copy)
                        f(PT[0:NS, 1312:1344], PS[0:NS, 3 * e, 288:320], ACT.Copy).then_inc(S["pt_a"], 1)
                    act.wait_ge(S["pv_mm"], l * 8 + 2 * hp + 2)
                    o = (2 + hp) * T
                    f(BH[:, o:o + NP_], PS[:, 1, 0:NP_], ACT.Copy)
                    f(BH[:, o + NP_:o + T], PS[:, 2, 0:NS], ACT.Copy).then_inc(S["pv_hi"], 1)

                act.wait_ge(S["st_kr"], (l + 1) * 16)

                def br(p, u, s, m):
                    if u == 0 or s == 0:
                        act.wait_ge(w_used[s], l * PAIRS_L + BASE["br"] + p + 2)
                        act.wait_ge(S["tf_free"], l * KC + m + 1)
                        f(two(LNT[2 * u + s]), banks2(2 * s), ACT.Tanh, scale=0.5).then_inc(bank_free[s], 1)
                    else:
                        act.wait_ge(S["m_ok"], l * KC + m + 1)
                        f(MXH[:, bass.ds(m * T, T)], LNT[3], ACT.Copy, scale=0.5).then_inc(S["mx_hi"], 1)
                load(MRAW[:, :], io["mem"], "mem_in")
                phase(l, "br", br, 2)
                for s in (0, 1):
                    act.wait_ge(w_used[s], l * PAIRS_L + BASE["wo"] + 1)
                load(MK[1][:, :], io["memk_in"][l], "cmem_in")
                load(MV[1][:, :], io["memv_in"][l], "cmem_in")
                act.wait_ge(S["mem_in"], (l + 1) * 16)
                f(MMH[:, :], MRAW[:, :], ACT.Copy).then_inc(S["mem_hi"], 1)
                phase(l, "wo", lambda p, u, s, q: square(4 * l + 1, p * 2 + s, s))
                n = 4 * l + 1
                ln_mean(n)
                for i, (name, p) in enumerate([(m, p) for m in ("memk", "memv") for p in range(4)]):
                    for s in (0, 1):
                        pair(l, name, p, s, p == 3)
                    if i == 0:
                        ln_rstd(n)
                    elif i < 5:
                        for c in (2 * i - 2, 2 * i - 1):
                            ln_chunk(n, 1, c)
                for s in (0, 1):
                    act.wait_ge(bank_free[s], l * USES_L + UBASE["memv"] + 3)
                act.dma_start(io["mem_k"][l], MK[0][:, :]).then_inc(S["st_mem"], 16)
                act.dma_start(io["mem_v"][l], MV[0][:, :]).then_inc(S["st_mem"], 16)

                for s in (0, 1):
                    pair(l, "cq", 0, s, False)
                for h in range(4):
                    act.wait_ge(S["cmx_ok"], l * 4 + h + 1)
                    c0 = 16 * (h % 2)
                    for i in range(4):
                        f(CP[h % 2][:, i * 256:(i + 1) * 256], PS[:, 4 + i // 2, (i % 2) * 256:(i % 2 + 1) * 256], ACT.Exp,
                          scale=MEM_SCALE, bias=SC[:, c0 + 5 + i:c0 + 6 + i], accum_out=SC[:, c0 + 10 + i:c0 + 11 + i])
                    f(CP[h % 2][0:NS, 1024:1280], PS[0:NS, 6, 0:256], ACT.Exp, scale=MEM_SCALE,
                      bias=SC[0:NS, c0 + 9:c0 + 10], accum_out=SC[0:NS, c0 + 14:c0 + 15])
                    act.drain().then_inc(S["cexp_ok"], 1)
                    if h < 3:
                        for s in (0, 1):
                            pair(l, "cq", h + 1, s, h == 2)
                    for c in (0, 1):
                        act.wait_ge(S["cpv_mm"], l * 8 + 2 * h + c + 1)
                        o = (2 * h + c) * T
                        bp, bs = CPV[h]
                        if c == 0:
                            f(OH[:, o:o + 2 * T].rearrange("p (c t) -> p c t", c=2)[:, :, NP_:T],
                              PS[:, bs, 0:2 * NS].rearrange("p (c t) -> p c t", c=2), ACT.Copy)
                        f(OH[:, o:o + NP_], PS[:, bp[c], 0:NP_], ACT.Copy).then_inc(S["cpv_hi"], 1)
                phase(l, "co", lambda p, u, s, q: square(4 * l + 2, p * 2 + s, s))
                layer_norm(4 * l + 2, 2)
                ffn_in(l, "f2i")
                ffn_out(l, "f2o", 4 * l + 3)
                layer_norm(4 * l + 3, 3)
            act.wait_ge(S["x_ready"], (4 * L + 1) * KC)
            act.dma_start(io["y"], Yf[:, :]).then_inc(S["st_y"], 16)
            act.wait_ge(S["st_y"], 16)

        @block.vector
        def _(ve):
            def tt(out, a, b, op):
                return ve.tensor_tensor(out, a, b, op)

            def stt(out, a, sc, b, op0, op1):
                return ve.scalar_tensor_tensor(out, a, sc, b, op0, op1)

            def group_done(l, name, p, s):
                ve.wait_ge(w_used[s], l * PAIRS_L + BASE[name] + p + 2)

            def residual(n, m, b, scale):
                y = Yf[:, bass.ds(m * T, T)]
                stt(two(y), banks2(2 * b), scale, two(y), ALU.mult, ALU.add).then_inc(bank_free[b], 1)
                ve.drain().then_inc(S["y_upd"], 1)
                tt(YS, YS, y, ALU.add)
                ve.wait_ge(S["y_sq"], n * KC + m + 1)
                tt(QS, QS, SQ[b], ALU.add).then_inc(S["q_add"], 1)

            def clear_sums():
                ve.memset(YS, 0.0)
                ve.memset(QS, 0.0)
                ve.drain()

            def ln_var(n):
                ve.drain().then_inc(S["stats_ready"], 1)
                ve.wait_ge(S["mean"], n + 1)
                tt(LNT[5], MEAN, MEAN, ALU.mult)
                ve.drain()
                stt(two(RSTD), banks2(6), 1.0 / D, two(LNT[5]), ALU.mult, ALU.subtract)
                ve.drain()
                ve.tensor_scalar(RSTD, RSTD, 0.0, EPS / ALPHA ** 2, ALU.max, ALU.add).then_inc(S["var"], 1)

            def ln_chunk(c):
                y = Yf[:, bass.ds(c * T, T)]
                tt(y, y, MEAN, ALU.subtract)
                ve.drain()
                tt(y, y, RSTD, ALU.mult).then_inc(S["ln_d"], 1)

            def layer_norm(n):
                ln_var(n)
                ve.wait_ge(S["rstd"], n + 1)
                settle(ve)
                with ve.Fori(0, KC) as c:
                    ln_chunk(c)

            ve.memset(XH[:, KC * T:].bitcast(F32), 0.0)
            ve.memset(XL[:, KC * T:].bitcast(F32), 0.0)
            ve.memset(SC[:, :], 1.0)
            for s in (0, 1):
                ve.sem_inc(bank_free[s], 1)
            ve.sem_inc(S["lv_sel"], 1)
            ve.sem_inc(S["br_rd"], 1)
            ve.sem_inc(S["tf_free"], 1)
            ve.sem_inc(S["q_add"], 2)
            ve.wait_ge(S["const_in"], 16 * 3)
            ve.tensor_copy(MASK[:, :], LN_[:, 0:1024])
            ve.drain()

            with ve.Fori(0, L) as l:
                ve.wait_ge(S["small_in"], (l + 1) * 16)
                settle(ve)
                def ffn_in(l, name):
                    with ve.Fori(0, FC) as p:
                        ve.wait_ge(bank_free[0], l * USES_L + UBASE[name] + p + 2)
                        group_done(l, name, p, 1)
                        h = bass.ds(p * T, T)
                        settle(ve)
                        ve.drain()
                        tt(two(LNT[3]), two(LNT[2]), banks2(2), ALU.mult).then_inc(bank_free[1], 1)
                        ve.drain()
                        ve.tensor_copy(HH[:, h], LNT[3])
                        ve.drain()
                        tt(HL[:, h], LNT[3], HH[:, h].bitcast(F32), ALU.subtract).then_inc(S["h_ready"], 1)

                def ffn_out(l, name, n):
                    clear_sums()
                    with ve.Fori(0, 4) as q:
                        for u in (0, 1):
                            group_done(l, name, q * 2 + u, 1)
                            residual(n, q * 2 + u, u, 0.5 / ALPHA)
                    layer_norm(n)

                def proj_out(l, name, n):
                    clear_sums()
                    with ve.Fori(0, 4) as p:
                        for s in (0, 1):
                            group_done(l, name, p, s)
                            residual(n, p * 2 + s, s, 1.0 / ALPHA)

                ffn_in(l, "f1i")
                clear_sums()
                with ve.Fori(0, 4) as q:
                    for u in (0, 1):
                        group_done(l, "f1o", q * 2 + u, 1)
                        residual(4 * l, q * 2 + u, u, 0.5 / ALPHA)
                layer_norm(4 * l)
                ve.memset(SB[:, :], 0.0)
                ve.memset(A[:, :], 0.0)
                ve.memset(AS[:, :], 0.0)
                for c in (0, 1):
                    ve.memset(U[:, c * UW:c * UW + HIST], 0.0)
                ve.drain().then_inc(S["z_in"], 1)

                for g in range(12):
                    p, s = g // 2, g % 2
                    group_done(l, "win", p, s)
                    src = banks2(2 * s)
                    if g < 2:
                        o = g * UW
                        ve.tensor_copy(U[:, o + HIST:o + HIST + TH], PS[:, 2 * s, 0:TH])
                        ve.tensor_copy(U[:, o + HIST + TH:o + HIST + NP_], PS[:, 2 * s + 1, 0:NP_ - TH])
                        i = ve.tensor_copy(U[:, o + UQ + HIST:o + UW], PS[:, 2 * s + 1, NP_ - TH:TH])
                    elif g < 4:
                        i = ve.tensor_copy(two(QL[:, s * T:(s + 1) * T]), src)
                    elif g < 6:
                        i = ve.tensor_copy(two(CK[:, s * NK:s * NK + T]), src)
                    elif g == 6:
                        ve.tensor_copy(two(GA[0:16, :]), PS[0:16, 0:2, 0:TH])
                        i = tt(two(LNT[4][64:128, :]), PS[64:128, 0:2, 0:TH], two(KCOS[64:128, :]), ALU.mult)
                    elif g == 7:
                        i = tt(two(LNT[5][64:128, :]), PS[64:128, 2:4, 0:TH], two(KSIN[64:128, :]), ALU.mult)
                        i.then_inc(bank_free[s], 1)
                        ve.drain()
                        tt(KR[64:128, 0:T], LNT[4][64:128, :], LNT[5][64:128, :], ALU.add).then_inc(S["kr_ready"], 1)
                        continue
                    elif g == 8:
                        i = ve.tensor_scalar(two(GQ[:, :]), src, 32.0 ** -0.5, None, ALU.mult)
                    elif g == 9:
                        i = ve.tensor_copy(two(GK[:, :]), src)
                    else:
                        ve.wait_ge(S["tanh_r"], l * 2 + s + 1)
                        i = stt(two(SG[:, s * T:(s + 1) * T]), two(LNT[s]), 1.0, src, ALU.add, ALU.mult)
                    i.then_inc(bank_free[s], 1)
                ve.wait_ge(S["hist_in"], (l + 1) * 32)
                settle(ve)
                ve.drain().then_inc(S["u_ready"], 1)
                U3 = U[:, :].rearrange("p (c t) -> p c t", c=2)
                W1 = LN_[:, 0:2 * UW].rearrange("p (c t) -> p c t", c=2)
                W2 = LN_[:, 2 * UW:4 * UW].rearrange("p (c t) -> p c t", c=2)
                O3 = O[:, :].rearrange("p (c t) -> p c t", c=2)
                tt(W1[:, :, 1:], U3[:, :, 1:], U3[:, :, :UW - 1], ALU.add)
                ve.drain()
                tt(W2[:, :, 3:], W1[:, :, 3:], W1[:, :, 1:UW - 2], ALU.add)
                ve.drain()
                tt(W1[:, 1, 7:], W2[:, 1, 7:], W2[:, 1, 3:UW - 4], ALU.add)
                ve.drain()
                tt(W2[64:128, 1, 15:], W1[64:128, 1, 15:], W1[64:128, 1, 7:UW - 8], ALU.add)
                ve.drain()
                for r, W in ((slice(0, 64), W1), (slice(64, 128), W2)):
                    for c in (0, 1):
                        for o, u0, n in ((0, HIST, NP_), (NP_, UQ + HIST, NS)):
                            stt(O3[r, c, o:o + n], W[r, c, u0:u0 + n], INVW[r, c:c + 1], U3[r, c, u0:u0 + n],
                                ALU.mult, ALU.subtract)
                ve.drain()
                for r, W in ((slice(0, 64), W1), (slice(64, 128), W2)):
                    tt(O3[r, :, 0:16], W[r, :, HIST:HIST + 16], INVC[r, :, :], ALU.mult)
                ve.drain()
                for r in (slice(0, 64), slice(64, 128)):
                    tt(O3[r, :, 0:16], O3[r, :, 0:16], U3[r, :, HIST:HIST + 16], ALU.subtract)
                ve.drain().then_inc(S["pooled"], 1)
                group_done(l, "gv", 0, 1)
                ve.tensor_copy(VT[:, 0:1024].rearrange("p (b t) -> p b t", b=2), PS[:, 4:6, :])
                ve.tensor_copy(VT[0:NS, 1024:1280], PS[0:NS, 6, 0:256]).then_inc(S["vt_ready"], 1)
                for i, (buf, w, g0) in enumerate(((QL, T, SM_QN), (CK, NK, SM_KN))):
                    ve.wait_ge(S["rq_mm"], 2 * l + i + 1)
                    ve.tensor_scalar(two(LNT[2]), banks2(6), 1.0 / 256, EPS, ALU.mult, ALU.add).then_inc(S["rq_v"], 1)
                    ve.wait_ge(S["rq_r"], 2 * l + i + 1)
                    for c in (0, 1):
                        b = buf[:, c * w:c * w + T]
                        j = stt(b, b, SMALL[:, g0 + c:g0 + c + 1], LNT[2], ALU.mult, ALU.mult)
                    j.then_inc(S["ck_in"], 1)
                for c in (0, 1):
                    ve.wait_ge(S["pool_hi"], l * 2 + c + 1)
                    j = stt(two(BL[:, c * T:(c + 1) * T]), banks2(2 * c), SMALL[:, SM_PS + c:SM_PS + c + 1],
                            two(BH[:, c * T:(c + 1) * T].bitcast(F32)), ALU.mult, ALU.subtract)
                j.then_inc(S["pool_lo"], 1)
                ve.wait_ge(S["z_abs"], l + 1)
                ve.tensor_scalar(two(LNT[5]), banks2(4), SMALL[:, SM_BA:SM_BA + 1], 0.0, ALU.add, ALU.min)
                ve.wait_ge(S["z_l"], l + 1)
                settle(ve)
                ve.drain()
                tt(LNT[3], LNT[5], LNT[4], ALU.subtract)
                ve.drain()
                ve.tensor_tensor_scan(LNT[0], RESET, LNT[3], 0.0, ALU.mult, ALU.add).then_inc(S["B_ok"], 1)
                ve.drain()
                B, EB, QD, KD, E, X = LNT

                def blocks(ap, w):
                    return ap.rearrange("p (n t) -> p n t", t=w)
                tt(blocks(KD[:, 0:NP_], 128), blocks(B[:, 0:NP_], 128)[:, :, 127:128].to_broadcast([128, 4, 128]),
                   blocks(B[:, 0:NP_], 128), ALU.subtract)
                tt(KD[:, NP_:T], B[:, T - 1:T].to_broadcast([128, NS]), B[:, NP_:T], ALU.subtract)
                ve.drain().then_inc(S["kd_sub"], 1)
                ve.wait_ge(S["eb_ok"], l + 1)
                tt(QD, GQ[:, :], EB, ALU.mult)
                ve.wait_ge(S["kdE"], l + 1)
                tt(KD, KD, GK[:, :], ALU.mult).then_inc(S["kd_ok"], 1)
                ve.wait_ge(S["kdt_mm"], l + 1)
                ve.tensor_copy(KDT[:, 0:512].rearrange("p (b t) -> p b t", b=4), PS[:, 0:4, 0:128])
                ve.tensor_copy(KDT[0:NS, 512:640], PS[0:NS, 4, 0:128]).then_inc(S["kdt_ok"], 1)
                ve.wait_ge(S["ds_mm"], l + 1)
                ve.wait_ge(S["gla_in"], (l + 1) * 64)
                for i in range(5):
                    dst, src, eb = (i, i - 1, i * 128 + 127) if i < 4 else (5, 4, T - 1)
                    for h in range(4):
                        r = slice(32 * h, 32 * h + 32)
                        d = SB[r, dst * 256 + h * 64:dst * 256 + (h + 1) * 64]
                        inc = PS[r, i, h * 64:(h + 1) * 64]
                        if i == 0:
                            ve.tensor_copy(d, inc)
                        else:
                            stt(d, SB[r, src * 256 + h * 64:src * 256 + (h + 1) * 64], EB[r, eb:eb + 1], inc, ALU.mult, ALU.add)
                    j = ve.drain()
                j.then_inc(S["sb_ok"], 1)

                def lv_sub(j):
                    b = LEVELS[j]
                    w = NP_ if j < 2 else T
                    Bv, Ev = blocks(B[:, 0:w], 2 * b), blocks(E[:, 0:w], 2 * b)
                    ref = Bv[:, :, b - 1:b].to_broadcast([128, w // (2 * b), b])
                    tt(Ev[:, :, 0:b], ref, Bv[:, :, 0:b], ALU.subtract)
                    tt(Ev[:, :, b:2 * b], Bv[:, :, b:2 * b], ref, ALU.subtract)
                    ve.drain().then_inc(S["lv_e"], 1)
                lv_sub(0)
                for j in range(8):
                    if j < 7:
                        b = LEVELS[j]
                        w = NP_ if j < 2 else T
                        ve.wait_ge(S["lv_E"], l * 7 + j + 1)
                        if j:
                            ve.wait_ge(S["lv_mm"], l * 8 + j)
                        Xv, Ev = blocks(X[:, 0:w], 2 * b), blocks(E[:, 0:w], 2 * b)
                        tt(Xv[:, :, 0:b], Ev[:, :, 0:b], blocks(GK[:, 0:w], 2 * b)[:, :, 0:b], ALU.mult)
                        tt(Xv[:, :, b:2 * b], Ev[:, :, b:2 * b], blocks(GQ[:, 0:w], 2 * b)[:, :, b:2 * b], ALU.mult)
                        ve.drain().then_inc(S["lv_x"], 1)
                        if j < 6:
                            lv_sub(j + 1)
                    ve.wait_ge(S["lv_mm"], l * 8 + j + 1)
                    settle(ve)
                    mk = MASK[:, j * 128:(j + 1) * 128]
                    for h in range(4):
                        ve.copy_predicated(blocks(A[:, h * NP_:(h + 1) * NP_], 128),
                                           mk.unsqueeze(1).to_broadcast([128, 4, 128]), blocks(PS[:, 4 + h, :], 128))
                        if j >= 2:
                            ve.copy_predicated(AS[0:NS, h * NS:(h + 1) * NS], mk[0:NS, 0:NS], PS[0:NS, h, 0:NS])
                    ve.drain().then_inc(S["lv_sel"], 1)
                ve.wait_ge(S["o_mm"], l + 1)
                ve.tensor_copy(O3[:, :, 0:NP_], PS[:, 4:6, :])
                ve.tensor_copy(O3[:, :, NP_:T], PS[:, 6:8, 0:NS])
                ve.drain().then_inc(S["o_ok"], 1)
                ve.wait_ge(S["o_ms"], l + 1)
                ve.tensor_scalar(LN_[:, 2 * T:4 * T].rearrange("p (b t) -> p b t", b=4), PS[:, 0:4, 0:TH], 1.0 / 64, EPS,
                                 ALU.mult, ALU.add).then_inc(S["o_v"], 1)
                ve.wait_ge(S["o_r"], l + 1)
                stt(O[:, :], O[:, :], SMALL[:, SM_GN:SM_GN + 1], LN_[:, 2 * T:4 * T], ALU.mult, ALU.mult)
                ve.drain()
                stt(O[:, :], O[:, :], 0.5, SG[:, :], ALU.mult, ALU.mult).then_inc(S["o_y"], 1)
                ve.wait_ge(S["o_hi"], l + 1)
                tt(BL[:, 6 * T:8 * T], O[:, :], BH[:, 6 * T:8 * T].bitcast(F32), ALU.subtract).then_inc(S["o_lo"], 1)

                ve.wait_ge(S["latr_hi"], l * 2 + 1)
                tt(QO[:, :], QL[:, :], QH[:, :].bitcast(F32), ALU.subtract)
                ve.wait_ge(S["latr_hi"], l * 2 + 2)
                tt(CO[:, 0:2 * NK], CK[:, :], CH[:, 0:2 * NK].bitcast(F32), ALU.subtract)
                ve.memset(CH[:, 2 * NK:].bitcast(F32), 0.0)
                ve.memset(CO[:, 2 * NK:].bitcast(F32), 0.0)
                ve.drain().then_inc(S["lat_ready"], 1)
                for e in (0, 1):
                    ve.memset(P[e][:, 0:1280], 0.0)
                    ve.tensor_copy(KT[e][64:128, :], KR[64:128, :])
                group_done(l, "vup", 0, 1)
                ve.tensor_copy(V[:, 0:2048].rearrange("p (b t) -> p b t", b=4), PS[:, 0:4, :]).then_inc(S["v_ok"], 1)
                for hp in range(4):
                    s = hp % 2
                    group_done(l, "mla", hp // 2, s)
                    for e in (0, 1):
                        j = tt(two(LNT[e]), banks2(2 * e), two(QTAB), ALU.mult)
                    j.then_inc(S["qk_ok"], 1)
                    for e in (0, 1):
                        h = 2 * hp + e
                        c0 = 16 * e
                        ve.wait_ge(S["sc_mm"], l * 8 + h + 1)
                        for i, bank, o in ((3, 0, 0), (2, 1, 0), (0, 1, 384), (1, 2, 0)):
                            for hf in (0, 1):
                                r = slice(64 * hf, 64 * hf + 64)
                                ve.reduce_max(SC[r, c0 + i:c0 + i + 1], PS[r, 3 * e + bank, o:o + 128 * i + 64 * (hf + 1)], AX.X)
                        ve.reduce_max(SC[0:NS, c0 + 4:c0 + 5], PS[0:NS, 3 * e + 2, 256:416], AX.X)
                        ve.drain()
                        ve.tensor_scalar(SC[:, c0 + 5:c0 + 10], SC[:, c0:c0 + 5], -MLA_SCALE, None, ALU.mult).then_inc(S["mx_ok"], 1)
                    for e in (0, 1):
                        h = 2 * hp + e
                        c0 = 16 * e
                        ve.wait_ge(S["exp_ok"], l * 8 + h + 1)
                        ve.reciprocal(SC[:, c0 + 10:c0 + 15], SC[:, c0 + 10:c0 + 15])
                        ve.drain()
                        for i in range(4):
                            po = 128 * (i * (i + 1) // 2)
                            b = P[e][:, po:po + 128 * (i + 1)]
                            ve.tensor_scalar(b, b, SC[:, c0 + 10 + i:c0 + 11 + i], None, ALU.mult)
                        b = P[e][0:NS, 1280:1440]
                        ve.tensor_scalar(b, b, SC[0:NS, c0 + 14:c0 + 15], None, ALU.mult).then_inc(S["p_ok"], 1)
                    for e in (0, 1):
                        h = 2 * hp + e
                        ve.wait_ge(S["pt_mm"], l * 8 + h + 1)
                        if e:
                            ve.wait_ge(S["pv_mm"], l * 8 + h)
                        ve.tensor_copy(PT[:, 0:512], PS[:, 6, :])
                        ve.tensor_copy(PT[:, 512:896], PS[:, 7, 0:384])
                        ve.tensor_copy(PT[:, 1152:1280], PS[:, 7, 384:512]).then_inc(S["pt_d"], 1)
                    ve.wait_ge(S["pv_hi"], l * 4 + hp + 1)
                    o = (2 + hp) * T
                    tt(BL[:, o:o + NP_], PS[:, 1, 0:NP_], BH[:, o:o + NP_].bitcast(F32), ALU.subtract)
                    tt(BL[:, o + NP_:o + T], PS[:, 2, 0:NS], BH[:, o + NP_:o + T].bitcast(F32), ALU.subtract).then_inc(S["pv_lo"], 1)

                with ve.Fori(0, KC) as m:
                    ve.wait_ge(w_used[1], l * PAIRS_L + BASE["br"] + m * 2 + 3)
                    ve.wait_ge(bank_free[1], l * USES_L + UBASE["br"] + m * 2 + 2)
                    ve.wait_ge(bank_free[0], l * USES_L + UBASE["br"] + m * 2 + 3)
                    settle(ve)
                    ve.drain()
                    stt(two(LNT[3]), two(LNT[0]), 1.0, banks2(4), ALU.add, ALU.mult)
                    stt(two(LNT[4]), two(LNT[1]), 1.0, banks2(6), ALU.add, ALU.mult).then_inc(S["br_rd"], 1)
                    stt(two(LNT[5]), two(LNT[2]), 1.0, banks2(2), ALU.add, ALU.mult).then_inc(bank_free[1], 1)
                    ve.drain().then_inc(S["tf_free"], 1)
                    tt(LNT[3], LNT[3], LNT[4], ALU.add)
                    ve.drain()
                    tt(LNT[3], LNT[3], LNT[5], ALU.add).then_inc(S["m_ok"], 1)
                    ve.wait_ge(S["mx_hi"], l * KC + m + 1)
                    x = bass.ds(m * T, T)
                    stt(MXL[:, x], LNT[3], 0.5, MXH[:, x].bitcast(F32), ALU.mult, ALU.subtract).then_inc(S["mx_lo"], 1)
                ve.wait_ge(S["mem_hi"], l + 1)
                tt(MML[:, :], MRAW[:, :], MMH[:, :].bitcast(F32), ALU.subtract).then_inc(S["mem_ready"], 1)
                proj_out(l, "wo", 4 * l + 1)
                ln_var(4 * l + 1)
                for p in range(4):
                    for s in (0, 1):
                        group_done(l, "memk", p, s)
                        o = (p * 2 + s) * NMEM
                        ve.tensor_copy(MK[0][:, o:o + NMEM], PS[:, 2 * s, 0:NMEM]).then_inc(bank_free[s], 1)
                    if p == 0:
                        ve.wait_ge(S["rstd"], 4 * l + 2)
                    for c in (2 * p, 2 * p + 1):
                        ln_chunk(c)
                for q in range(2):
                    for u in (0, 1):
                        group_done(l, "memv", q * 2 + u, 1)
                        for t in (0, 1):
                            o = (q * 2 + u) * 256 + t * D
                            i = ve.tensor_copy(MV[0][:, o:o + 256], PS[:, 2 * u, t * 256:(t + 1) * 256])
                        i.then_inc(bank_free[u], 1)

                def queries(h, s):
                    group_done(l, "cq", h, s)
                    ve.tensor_copy(two(LNT[s]), banks2(2 * s)).then_inc(bank_free[s], 1)
                for s in (0, 1):
                    queries(0, s)
                for h in range(4):
                    c0 = 16 * (h % 2)
                    ve.wait_ge(S["csc_mm"], l * 4 + h + 1)
                    ve.reduce_max(SC[:, c0:c0 + 4], PS[:, 4:6, :].rearrange("p b (i t) -> p (b i) t", i=2), AX.X)
                    ve.reduce_max(SC[0:NS, c0 + 4:c0 + 5], PS[0:NS, 6, 0:256], AX.X)
                    ve.drain()
                    ve.tensor_scalar(SC[:, c0 + 5:c0 + 10], SC[:, c0:c0 + 5], -MEM_SCALE, None, ALU.mult).then_inc(S["cmx_ok"], 1)
                    ve.wait_ge(S["cexp_ok"], l * 4 + h + 1)
                    ve.reciprocal(SC[:, c0 + 10:c0 + 15], SC[:, c0 + 10:c0 + 15])
                    ve.drain()
                    for i in range(4):
                        b = CP[h % 2][:, i * 256:(i + 1) * 256]
                        ve.tensor_scalar(b, b, SC[:, c0 + 10 + i:c0 + 11 + i], None, ALU.mult)
                    b = CP[h % 2][0:NS, 1024:1280]
                    ve.tensor_scalar(b, b, SC[0:NS, c0 + 14:c0 + 15], None, ALU.mult).then_inc(S["cp_ok"], 1)
                    if h < 3:
                        queries(h + 1, 0)
                    ve.wait_ge(S["cpt_mm"], l * 4 + h + 1)
                    ve.tensor_copy(CPT[:, 0:NP_], PS[:, 7, :])
                    ve.tensor_copy(CPT[:, T:T + NP_], PS[:, 4, :])
                    ve.tensor_copy(CPT[:, :].rearrange("p (k t) -> p k t", k=2)[:, :, NP_:T],
                                   PS[:, 6, 0:2 * NS].rearrange("p (k t) -> p k t", k=2)).then_inc(S["cpt_d"], 1)
                    if h < 3:
                        queries(h + 1, 1)
                    bp, bs = CPV[h]
                    for c in (0, 1):
                        ve.wait_ge(S["cpv_hi"], l * 8 + 2 * h + c + 1)
                        o = (2 * h + c) * T
                        if c == 0:
                            hi, lo_ = (x[:, o:o + 2 * T].rearrange("p (c t) -> p c t", c=2)[:, :, NP_:T] for x in (OH, OL))
                            tt(lo_, PS[:, bs, 0:2 * NS].rearrange("p (c t) -> p c t", c=2), hi.bitcast(F32), ALU.subtract)
                        tt(OL[:, o:o + NP_], PS[:, bp[c], 0:NP_], OH[:, o:o + NP_].bitcast(F32),
                           ALU.subtract).then_inc(S["cpv_lo"], 1)
                proj_out(l, "co", 4 * l + 2)
                layer_norm(4 * l + 2)

                ve.wait_ge(S["st_mem"], (l + 1) * 32)
                settle(ve)
                ffn_in(l, "f2i")
                ffn_out(l, "f2o", 4 * l + 3)


def tiles_of(w):
    l, k, m = w.shape
    return w.reshape(l, k // 128, 128, m // 128, 128).transpose(0, 3, 2, 1, 4)


def groups(w):
    t = tiles_of(w)
    return np.ascontiguousarray(t).reshape(t.shape[0], t.shape[1], 128, -1)


def feat(a):
    *lead, t, d = a.shape
    n = len(lead)
    a = a.reshape(*lead, t, d // 128, 128)
    return np.ascontiguousarray(a.transpose(*range(n), n + 2, n + 1, n)).reshape(*lead, 128, -1)


def unfeat(a, t):
    *lead, p, ct = a.shape
    n = len(lead)
    a = a.reshape(*lead, 128, ct // t, t)
    return np.ascontiguousarray(a.transpose(*range(n), n + 2, n + 1, n)).reshape(*lead, t, -1)


def constants():
    half = 16
    inv = (np.float32(10000.0) ** (-np.arange(half, dtype=np.float32) / np.float32(half))).astype(np.float32)
    pos = np.concatenate([np.arange(NP_), PAST + np.arange(NS)]).astype(np.float32)
    ang = (pos[None, :] * inv[:, None]).astype(np.float32)
    cos, sin = np.cos(ang), np.sin(ang)
    c2, s2 = np.concatenate([cos, cos]), np.concatenate([-sin, sin])
    one, zero = np.ones((64, T), np.float32), np.zeros((64, T), np.float32)
    reset = np.ones((128, T), np.float32)
    reset[:, 0::128] = 0
    tab = np.concatenate([np.concatenate([one, c2, s2]), np.concatenate([zero, c2, c2]),
                          np.concatenate([zero, s2, s2]), reset], 1).astype(np.float32)
    cst = np.zeros((128, 3 * 128 + 34), np.float32)
    cst[:, 0:128] = np.eye(128)
    cst[:, 128:256] = 1
    cst[0:64, 256:320] = 1
    cst[64:128, 320:384] = 1
    win = np.array([[2, 8], [4, 16]])
    for r in (0, 1):
        for c in (0, 1):
            cst[64 * r:64 * r + 64, 384 + 16 * c:400 + 16 * c] = 1.0 / np.minimum(np.arange(16) + 1, win[r, c])
            cst[64 * r:64 * r + 64, 416 + c] = 1.0 / win[r, c]
    s, t = np.meshgrid(np.arange(128), np.arange(128), indexing="ij")
    mask = [(s // (2 * b) == t // (2 * b)) & (s % (2 * b) < b) & (t % (2 * b) >= b) for b in LEVELS] + [s == t]
    mask = np.concatenate([m.astype(np.float32) for m in mask], 1)
    return tab, cst, np.ascontiguousarray(mask)


def layout(a):
    a = {k: np.asarray(v) for k, v in a.items()}
    f32 = np.float32
    d = {}
    d["x"] = feat(np.concatenate([a["x_prompt"][0], a["x_sample"][0]], 0))
    d["mem"] = feat(a["mem_prompt"][0])
    d["tab"], d["cst"], d["mask"] = constants()
    d["memk"] = groups(a["mem_w_k"])
    def moving(w, cols):
        l, k, m = w.shape
        return np.ascontiguousarray(w.reshape(l, k // 512, 4, 128, m // cols, cols).transpose(0, 4, 1, 3, 2, 5)).reshape(
            l, (m // cols) * (k // 512), 128, 4 * cols)
    d["memv"] = moving(a["mem_w_v"], 256)
    for n, wi, wo in (("f1", "w_ffn1_in", "w_ffn1_out"), ("f2", "w_ffn2_in", "w_ffn2_out")):
        t = groups(a[wi])
        d[n + "i"] = np.ascontiguousarray(t.reshape(L, 2, FC, 128, -1).transpose(0, 2, 1, 3, 4)).reshape(L, 2 * FC, 128, -1)
        t = tiles_of(a[wo])
        d[n + "o"] = np.ascontiguousarray(t.reshape(L, KC, 128, 2, 11, 128).transpose(0, 1, 3, 2, 4, 5)).reshape(
            L, 2 * KC, 128, -1)
    w = a["w_in"]
    cuts = np.cumsum([0, 256, 256, 256, 32, 128, 128, 256, 16, 256, 3072])
    pool, ql, ck, kr, gq, gk, gv, ga, gr, gates = (w[:, :, i:j] for i, j in zip(cuts, cuts[1:]))
    swap = np.concatenate([kr[:, :, 16:], kr[:, :, :16]], 2)
    z48, z64 = np.zeros((L, D, 48), f32), np.zeros((L, D, 64), f32)
    d["win"] = groups(np.concatenate([pool, ql, ck, ga, z48, kr, kr, z64, swap, swap, gq, gk, gr], 2))
    d["gv"] = moving(gv, 256)
    uq = a["mla_w_uq"].reshape(L, 256, 8, 96)
    uq = np.concatenate([uq[..., :64], uq[..., 64:], uq[..., 80:96], uq[..., 64:80]], -1).reshape(L, 256, 1024)
    uqt = tiles_of(uq)
    ukt = tiles_of(a["mla_w_uk"].reshape(L, 256, 512))
    q4 = uqt.reshape(L, 4, 2, 128, 256).transpose(0, 1, 3, 2, 4).reshape(L, 4, 128, 512)
    d["mla"] = np.ascontiguousarray(np.concatenate([q4, ukt.reshape(L, 4, 128, 256)], 3))
    d["vup"] = np.ascontiguousarray(a["mla_w_uv"].reshape(L, 2, 128, 512))
    g3 = groups(gates).reshape(L, 3, KC, 128, -1).transpose(0, 2, 1, 3, 4)
    b = groups(np.concatenate([a["w_branch_pool"], a["w_branch_mla"], a["w_branch_gla"]], 1))
    d["br"] = np.ascontiguousarray(np.concatenate([g3, b[:, :, None]], 2)).reshape(L, 4 * KC, 128, -1)
    d["wo"], d["cq"], d["co"] = groups(a["w_out"]), groups(a["mem_w_q"]), groups(a["mem_w_o"])

    sm = np.zeros((L, 128, SM_W), f32)
    sm[:, :, SM_LNG:SM_LNG + 32] = a["ln_g"].reshape(L, 32, 128).transpose(0, 2, 1)
    sm[:, :, SM_LNB:SM_LNB + 32] = a["ln_b"].reshape(L, 32, 128).transpose(0, 2, 1)
    for o, n in ((SM_PS, "pool_scale"), (SM_QN, "mla_q_norm"), (SM_KN, "mla_kv_norm")):
        sm[:, :, o:o + 2] = a[n].reshape(L, 2, 128).transpose(0, 2, 1)
    sm[:, :, SM_BA] = a["gla_b_a"]
    sm[:, :, SM_GN] = np.concatenate([a["gla_norm"], a["gla_norm"]], 1)
    for g in range(4):
        r = 64 * (g % 2)
        c = SM_PW + 128 * (g // 2) + r
        sm[:, r:r + 64, c:c + 64] = a["pool_w"][:, g]
    sm[:, 0:16, SM_WA:SM_WA + 128] = a["gla_w_a2"]
    d["small"] = sm
    d["pool_in"] = feat(a["cache_pool"][:, 0])
    d["ckv_in"] = feat(a["cache_mla_ckv"][:, 0])
    d["krope_in"] = np.ascontiguousarray(a["cache_mla_krope"][:, 0].transpose(0, 2, 1))
    d["gla_in"] = np.ascontiguousarray(a["state_gla"][:, 0].reshape(L, 128, 64))
    d["memk_in"] = feat(a["cache_mem_k"][:, 0].reshape(L, NMEM, D))
    d["memv_in"] = np.ascontiguousarray(a["cache_mem_v"][:, 0].reshape(L, 2, 128, D).transpose(0, 2, 1, 3)).reshape(L, 128, 2 * D)
    return d


OUTS = {"y": (128, KC * T), "pool_p": (L, 128, 2 * HIST), "pool_s": (L, 128, 2 * HIST), "ckv": (L, 128, 2 * T),
        "krope": (L, 32, T), "gla_p": (L, 128, 64), "gla_s": (L, 128, 64), "mem_k": (L, 128, KC * NMEM),
        "mem_v": (L, 128, 2 * D)}


def kernel(**inputs):
    import concourse.bacc as bacc
    from concourse.bass_utils import run_bass_kernel_spmd

    arrays = layout(inputs)
    nc = bacc.Bacc("TRN2", target_bir_lowering=False, num_devices=1)
    io = {}
    for n, v in arrays.items():
        io[n] = nc.dram_tensor("in_" + n, v.shape, mybir.dt.from_np(v.dtype), kind="ExternalInput").ap()
    for n, shape in OUTS.items():
        io[n] = nc.dram_tensor("out_" + n, shape, F32, kind="ExternalOutput").ap()
    build(nc, io)
    r = run_bass_kernel_spmd(nc, [{"in_" + n: v for n, v in arrays.items()}], core_ids=[0]).results[0]
    o = {n: np.asarray(r["out_" + n]) for n in OUTS}
    y = unfeat(o["y"], T)
    ckv = unfeat(o["ckv"], T)
    kr = o["krope"].transpose(0, 2, 1)
    mk = unfeat(o["mem_k"], NMEM).reshape(L, 1, NMEM, 4, 256)
    mv = np.ascontiguousarray(o["mem_v"].reshape(L, 128, 2, D).transpose(0, 2, 1, 3)).reshape(L, 1, NMEM, 4, 256)
    c = np.ascontiguousarray
    return (c(y[None, :NP_]), c(y[None, NP_:]),
            unfeat(o["pool_p"], HIST)[:, None], unfeat(o["pool_s"], HIST)[:, None],
            c(ckv[:, None, :NP_]), c(ckv[:, None, NP_:]), c(kr[:, None, :NP_]), c(kr[:, None, NP_:]),
            o["gla_p"].reshape(L, 1, 4, 32, 64), o["gla_s"].reshape(L, 1, 4, 32, 64), mk, mv)
```

```python
from contextlib import ExitStack

import numpy as np

import concourse.bass as bass
from concourse import mybir

F32 = mybir.dt.float32
F32R = mybir.dt.float32r
U8 = mybir.dt.uint8
ALU = mybir.AluOpType
ACT = mybir.ActivationFunctionType
AX = mybir.AxisListType

D = 1024
KC = D // 128
NP_, NS = 512, 32
T = NP_ + NS
TH = T // 2
PAST = 128
NMEM = 256
L = 2
DFF = 2816
FC = DFF // 128
PAD = 96
EPS = 1e-5
ALPHA = (2 * L) ** 0.25
HIST = 15
MLA_SCALE = (64 + 32) ** -0.5
MEM_SCALE = 256 ** -0.5
NK = T + PAST
KH = NK // 2
LEVELS = (64, 32, 16, 8, 4, 2, 1)

PHASES = [("f1i", 22, 8), ("f1o", 8, 11), ("win", 6, 8),
          ("vup", 1, 4), ("mla", 2, 6), ("gv", 1, 8), ("ab", 8, 11), ("cg", 4, 10), ("wo", 4, 8), ("memk", 4, 8), ("memv", 4, 8),
          ("cq", 4, 8), ("co", 4, 8),
          ("f2i", 22, 8), ("f2o", 8, 11)]
PAIRS = {n: p for n, p, _ in PHASES}
TILES = {n: t for n, _, t in PHASES}
BASE = {}
for _n, _p, _ in PHASES:
    BASE[_n] = sum(PAIRS[m] for m in BASE)
NEXT = {a[0]: b[0] for a, b in zip(PHASES, PHASES[1:] + PHASES[:1])}
PAIRS_L = sum(PAIRS.values())
USES = [("f1i", 22), ("f1o", 4), ("win", 6), ("cg", 4), ("wo", 4), ("memk", 4), ("memv", 2), ("cq", 4),
        ("co", 4), ("f2i", 22), ("f2o", 4)]
UBASE = {}
_t = 0
for _n, _u in USES:
    UBASE[_n] = _t
    _t += _u
USES_L = _t
SM_LNG, SM_LNB, SM_PS, SM_QN, SM_KN, SM_BA, SM_GN, SM_PW, SM_WA = 0, 32, 64, 66, 68, 70, 71, 72, 328
SM_W = 456


def build(nc, io):
    with ExitStack() as ctx:
        at = [(nc.sbuf_base + 31) // 32 * 32]

        def place(name, cols, dt=F32, size=4):
            t = nc.alloc_sbuf_tensor_at(name, [128, cols], dt, offset=at[0])
            at[0] += (cols * size + 31) // 32 * 32
            return t

        def sem(name):
            return ctx.enter_context(nc.semaphore(name))

        XH = place("XH", KC * T + PAD, F32R)
        XL = place("XL", KC * T + PAD, F32R)
        Yf = place("Y", KC * T)
        Y = Yf[:, :].rearrange("p (c t) -> p c t", c=KC)
        WR = [place(f"WR{s}", 11 * 128) for s in (0, 1)]
        WH = [place(f"WH{s}", 11 * 128, F32R) for s in (0, 1)]
        WL = [place(f"WL{s}", 11 * 128, F32R) for s in (0, 1)]
        SMALL = place("SMALL", SM_W)
        TAB = place("TAB", 4 * T)
        QTAB, KCOS, KSIN, RESET = (TAB[:, i * T:(i + 1) * T] for i in range(4))
        CST = place("CST", 3 * 128 + 34)
        IDENT, ONES, BLK = (CST[:, i * 128:(i + 1) * 128] for i in range(3))
        INVC = CST[:, 384:416].rearrange("p (c t) -> p c t", c=2)
        INVW = CST[:, 416:418]
        MASK = place("MASK", 8 * 128, U8, 1)
        SC = place("SC", 32)
        LN_ = place("LNT", 6 * T)
        LNT = [LN_[:, i * T:(i + 1) * T] for i in range(6)]
        KT = [LN_[:, 2 * T + e * NK:2 * T + (e + 1) * NK] for e in (0, 1)]
        YS, QS, MEAN, RSTD = LNT[0], LNT[1], LNT[2], LNT[3]
        SQ = LNT[4:6]
        UW = 2 * HIST + T
        UQ = HIST + NP_
        W0 = at[0]

        HH = place("HH", FC * T, F32R)
        HL = place("HL", FC * T, F32R)
        end = at[0]
        at[0] = W0
        BH = place("BH", KC * T, F32R)
        BL = place("BL", KC * T, F32R)
        R0 = at[0]
        QL = place("QL", 2 * T)
        CK = place("CK", 2 * NK)
        KR = place("KR", NK)
        GA = place("GA", T)
        B = GA[:, 0:T]
        R1 = at[0]
        at[0] = R0 + 2 * KC * T * 4
        TAIL = at[0]
        U = place("U", 2 * (2 * HIST + T))
        UP = place("UP", 2 * T)
        assert at[0] <= end
        off = [W0 + 6 * T * 4, W0 + 7 * T * 4, W0 + KC * T * 4 + 6 * T * 4]
        GQ, GK = (nc.alloc_sbuf_tensor_at(n, [128, T], F32, offset=o) for n, o in zip(("GQ", "GK"), off))
        SG = nc.alloc_sbuf_tensor_at("SG", [128, 2 * T], F32, offset=off[2])
        at[0] = R1
        QH = place("QH", 2 * T, F32R)
        QO = place("QO", 2 * T, F32R)
        CH = place("CH", 2 * NK + PAD, F32R)
        CO = place("CO", 2 * NK + PAD, F32R)
        V = place("V", 6 * 512)
        PW = 1280 + 160
        P1 = place("P1", PW)
        PT = place("PT", 1280 + 64)
        assert at[0] <= end
        P0 = nc.alloc_sbuf_tensor_at("P0", [128, PW], F32, offset=R0)
        P = [P0, P1]
        at[0] = R0
        A = place("A", 4 * NP_)
        AS = place("AS", 4 * NS)
        KDT = place("KDT", 5 * 128)
        assert at[0] <= R1 - T * 4
        at[0] = TAIL
        VT = place("VT", 5 * 256)
        SB = place("SB", 6 * 256)
        O = place("O", 2 * T)
        MT = place("MT", T)
        assert at[0] <= end
        at[0] = R0
        MXH = place("MXH", KC * T, F32R)
        MIX = nc.alloc_sbuf_tensor_at("MIX", [128, KC * T], F32, offset=at[0])
        MXL = place("MXL", KC * T, F32R)
        MRAW = place("MRAW", KC * NMEM)
        MMH = place("MMH", KC * NMEM, F32R)
        MML = place("MML", KC * NMEM, F32R)
        assert at[0] <= end
        at[0] = W0
        MK = [place("MKp", KC * NMEM), place("MKs", KC * NMEM)]
        MV = [place("MVp", 2 * D), place("MVs", 2 * D)]
        CP = [place("CP0", 1280), place("CP1", 1280)]
        CPT = place("CPT", 2 * T)
        OH = place("OH", KC * T, F32R)
        OL = place("OL", KC * T, F32R)
        assert at[0] <= end

        PS = ctx.enter_context(nc.psum_tensor("PS", [128, 8, 512], F32))

        def banks2(b, n=TH):
            return PS[:, b:b + 2, 0:n]

        def two(ap):
            return ap.rearrange("p (h t) -> p h t", h=2)

        CPV = [((0, 7), 1)] * 3 + [((5, 7), 6)]

        landed = [sem(f"w_landed{s}") for s in (0, 1)]
        hi_ready = [sem(f"w_hi{s}") for s in (0, 1)]
        lo_ready = [sem(f"w_lo{s}") for s in (0, 1)]
        w_used = [sem(f"w_used{s}") for s in (0, 1)]
        bank_free = [sem(f"bank_free{s}") for s in (0, 1)]
        names = ("const_in small_in x_in0 x_in1 x_in2 x_in3 x_hi x_ready x_done mem_in mem_hi mem_ready memk_out memv_out mem_st "
                 "silu h_ready y_upd y_sq q_add stats_ready stats_mm mean msq var rstd ln_d "
                 "hist_in caches_in gla_in u_ready pool_done pool_s pooled pool_mm pool_hi pool_lo kr_ready "
                 "rq_sq rq_mm rq_v rq_r ck_in latr_hi lat_ready tanh_r sg_done gv_mm vt_ready z_in z_mm z_abs z_l la_ok B_ok eb_ok kdE kd_sub kd_ok "
                 "kdt_mm kdt_ok ds_mm sb_ok lv_e lv_x lv_E lv_mm lv_sel o_mm o_ok o_sq o_ms o_v o_r o_y o_hi o_lo "
                 "v_mm v_ok krt qk_ok sc_mm mx_ok exp_ok p_ok pt_mm pt_a pt_d pv_mm pv_hi pv_lo "
                 "ga_mm ta_ok pl_mm pl_rd gb_mm tb_ok ml_rd smp_mm smp_sel tc_ok m_ok mx_hi mx_lo "
                 "cmem_in cq_ok csc_mm cmx_ok cexp_ok cp_ok cpt_mm cpt_d cpv_mm cpv_hi cpv_lo "
                 "st_pool st_ck st_kr st_gla st_mem st_y waited").split()
        S = {n: sem(n) for n in names}

        def settle(eng):
            eng.sem_inc(S["waited"], 1)
        block = ctx.enter_context(nc.Block())

        @block.sync
        def _(sp):
            with sp.Fori(0, L) as l:
                for name, pairs, tiles in PHASES:
                    with sp.Fori(0, pairs) as p:
                        c = l * PAIRS_L + BASE[name] + p
                        for s in (0, 1):
                            sp.wait_ge(lo_ready[s], c + 1)
                            sp.dma_start(WR[s][:, 0:tiles * 128], io[name][l, p * 2 + s]).then_inc(landed[s], 16)
            for s in (0, 1):
                sp.wait_ge(lo_ready[s], L * PAIRS_L + 1)
                sp.dma_start(WR[s][:, 0:TILES["f1i"] * 128], io["f1i"][0, s]).then_inc(landed[s], 16)

        @block.gpsimd
        def _(pool):
            for s in (0, 1):
                pool.sem_inc(lo_ready[s], 1)

            def lo(s, tiles, c):
                pool.wait_ge(hi_ready[s], c + 1)
                n = tiles * 128
                pool.tensor_tensor(WL[s][:, 0:n], WR[s][:, 0:n], WH[s][:, 0:n].bitcast(F32),
                                   ALU.subtract).then_inc(lo_ready[s], 1)

            def phase(l, name):
                n = PAIRS[name]
                base = l * PAIRS_L + BASE[name]
                if n > 1:
                    with pool.Fori(0, n - 1) as p:
                        for s in (0, 1):
                            lo(s, TILES[name], base + p + 1)
                for s in (0, 1):
                    lo(s, TILES[NEXT[name]], base + n)

            def x_lo_chunk(count, c):
                pool.wait_ge(S["x_hi"], count * KC + c + 1)
                xs = bass.ds(c * T, T)
                pool.tensor_tensor(XL[:, xs], Yf[:, xs], XH[:, xs].bitcast(F32),
                                   ALU.subtract).then_inc(S["x_ready"], 1)

            def x_lo(count):
                with pool.Fori(0, KC) as c:
                    x_lo_chunk(count, c)

            for s in (0, 1):
                lo(s, TILES["f1i"], 0)
            x_lo(0)
            with pool.Fori(0, L) as l:
                for name in ("f1i", "f1o"):
                    phase(l, name)
                x_lo(4 * l + 1)
                for name in ("win", "vup", "mla", "gv", "ab", "cg", "wo"):
                    phase(l, name)
                for i, (name, p) in enumerate([(n, p) for n in ("memk", "memv") for p in range(4)]):
                    for s in (0, 1):
                        lo(s, TILES["memk"], l * PAIRS_L + BASE[name] + p + 1)
                    if 1 <= i < 5:
                        for c in (2 * i - 2, 2 * i - 1):
                            x_lo_chunk(4 * l + 2, c)
                for name in ("cq", "co"):
                    phase(l, name)
                x_lo(4 * l + 3)
                phase(l, "f2i")
                phase(l, "f2o")
                x_lo(4 * l + 4)

        @block.tensor
        def _(pe):
            for s in (0, 1):
                pe.sem_inc(w_used[s], 1)

            def mm(out, lhsT, rhs, start, stop):
                return pe.matmul(out, lhsT, rhs, start=start, stop=stop, skip_group_check=True)

            def gemm(s, c, tiles, start=True, stop=True):
                pe.wait_ge(hi_ready[s], c + 1)
                for i, outs, first, last in tiles:
                    w = WH[s][:, i * 128:(i + 1) * 128]
                    for out, xh, xl in outs:
                        mm(out, w, xh, start and first, False)
                    for out, xh, xl in outs:
                        mm(out, w, xl, False, False)
                pe.wait_ge(lo_ready[s], c + 2)
                for i, outs, first, last in tiles:
                    w = WL[s][:, i * 128:(i + 1) * 128]
                    for out, xh, xl in outs:
                        m = mm(out, w, xh, False, stop and last)
                m.then_inc(w_used[s], 1)

            def halves(b, H, Lo, k, n=TH, width=T):
                return [(PS[:, b + h, 0:n], H[:, k * width + h * n:k * width + (h + 1) * n],
                         Lo[:, k * width + h * n:k * width + (h + 1) * n]) for h in (0, 1)]

            def chunk_tiles(b, H, Lo, ks=range(KC)):
                ks = list(ks)
                return [(i, halves(b, H, Lo, k), i == 0, i == len(ks) - 1) for i, k in enumerate(ks)]

            def first_pair(l, name, n, ready="x_ready", H=XH, Lo=XL):
                c = l * PAIRS_L + BASE[name]
                for s in (0, 1):
                    pe.wait_ge(bank_free[s], l * USES_L + UBASE[name] + 1)
                    pe.wait_ge(lo_ready[s], c + 2)
                for k in range(KC):
                    pe.wait_ge(S[ready], n * KC + k + 1)
                    for s in (0, 1):
                        wh, wl = (W[s][:, k * 128:(k + 1) * 128] for W in (WH, WL))
                        outs = halves(2 * s, H, Lo, k)
                        for out, xh, xl in outs:
                            mm(out, wh, xh, k == 0, False)
                        for out, xh, xl in outs:
                            mm(out, wh, xl, False, False)
                        for out, xh, xl in outs:
                            m = mm(out, wl, xh, False, k == KC - 1)
                        if k == KC - 1:
                            m.then_inc(w_used[s], 1)

            def standard(l, name, H, Lo, start=0, stop=None):
                with pe.Fori(start, stop or PAIRS[name]) as p:
                    for s in (0, 1):
                        pe.wait_ge(bank_free[s], l * USES_L + UBASE[name] + p + 1)
                        gemm(s, l * PAIRS_L + BASE[name] + p, chunk_tiles(2 * s, H, Lo))

            def ffn_out(l, name, n):
                pe.wait_ge(S["h_ready"], n * FC + 11)
                settle(pe)
                with pe.Fori(0, PAIRS[name] // 2) as q:
                    for u in (0, 1):
                        pe.wait_ge(bank_free[u], l * USES_L + UBASE[name] + q + 1)
                        for s in (0, 1):
                            c = l * PAIRS_L + BASE[name] + q * 2 + u
                            ks = range(11 * s, 11 * s + 11)
                            if s:
                                pe.wait_ge(S["h_ready"], (n + 1) * FC)
                            gemm(s, c, chunk_tiles(2 * u, HH, HL, ks), start=s == 0, stop=s == 1)

            def ln_stats(l, j):
                pe.wait_ge(S["stats_ready"], l * 4 + j + 1)
                for b, src in ((4, YS), (6, QS)):
                    for h in (0, 1):
                        m = mm(PS[:, b + h, 0:TH], ONES, src[:, h * TH:(h + 1) * TH], True, True)
                m.then_inc(S["stats_mm"], 1)

            def rms_stats(b, sq):
                for h in (0, 1):
                    for c in (0, 1):
                        m = mm(PS[:, b + h, 0:TH], ONES, sq[:, c * T + h * TH:c * T + (h + 1) * TH], c == 0, c == 1)
                return m

            pe.wait_ge(S["const_in"], 16 * 3)
            with pe.Fori(0, L) as l:
                first_pair(l, "f1i", 4 * l)
                standard(l, "f1i", XH, XL, 1)
                ffn_out(l, "f1o", l * 2 + 0)
                ln_stats(l, 0)

                first_pair(l, "win", 4 * l + 1)
                standard(l, "win", XH, XL, 1, 4)
                pe.wait_ge(bank_free[0], l * USES_L + UBASE["win"] + 5)
                for h in (0, 1):
                    m = mm(PS[:, 4 + h, 0:TH], SMALL[0:16, SM_WA:SM_WA + 128], GA[0:16, h * TH:(h + 1) * TH], True, True)
                m.then_inc(S["z_mm"], 1)
                pe.wait_ge(S["rq_sq"], l * 2 + 1)
                rms_stats(6, LN_[:, 0:2 * T]).then_inc(S["rq_mm"], 1)
                standard(l, "win", XH, XL, 4, 5)
                pe.wait_ge(S["pooled"], l + 1)
                pe.wait_ge(S["B_ok"], l + 1)
                for h in (0, 1):
                    m = mm(PS[:, 4 + h, 0:TH], SMALL[:, SM_PW:SM_PW + 128], UP[:, h * TH:(h + 1) * TH], True, True)
                m.then_inc(S["pool_mm"], 1)
                pe.wait_ge(S["rq_v"], l * 2 + 1)
                pe.wait_ge(S["rq_sq"], l * 2 + 2)
                rms_stats(6, LN_[:, 0:2 * T]).then_inc(S["rq_mm"], 1)
                standard(l, "win", XH, XL, 5, 6)
                pe.wait_ge(S["pool_lo"], l * 2 + 1)
                for h in (0, 1):
                    m = mm(PS[:, 4 + h, 0:TH], SMALL[:, SM_PW + 128:SM_PW + 256], UP[:, T + h * TH:T + (h + 1) * TH],
                           True, True)
                m.then_inc(S["pool_mm"], 1)

                pe.wait_ge(S["lat_ready"], l + 1)
                for s in (0, 1):
                    pe.wait_ge(bank_free[s], l * USES_L + UBASE["win"] + 7)
                cv = l * PAIRS_L + BASE["vup"]
                for s in (0, 1):
                    for part, W, ready in ((0, WH, hi_ready), (1, WL, lo_ready)):
                        pe.wait_ge(ready[s], cv + 1 + part)
                        for t in range(6):
                            if s == 0 and part == 0 and t == 4:
                                pe.wait_ge(S["pool_lo"], l * 2 + 2)
                            o = s * NK + t * 128
                            m = mm(PS[:, t, 0:512], CH[:, o:o + 128], W[s][:, 0:512], s == 0 and part == 0, s == 1 and part == 1)
                            if part == 0:
                                m = mm(PS[:, t, 0:512], CO[:, o:o + 128], W[s][:, 0:512], False, False)
                    m.then_inc(w_used[s], 1)
                pe.wait_ge(S["v_ok"], l * 2 + 2)
                for hp in range(4):
                    s = hp % 2
                    c = l * PAIRS_L + BASE["mla"] + hp // 2
                    if hp:
                        pe.wait_ge(S["pv_lo"], l * 4 + hp)
                    gemm(s, c, [(2 * e + k, halves(2 * e, QH, QO, k), k == 0, k == 1) for e in (0, 1) for k in (0, 1)]
                         + [(4 + k, halves(4, CH, CO, k, KH, NK), k == 0, k == 1) for k in (0, 1)])
                    pe.wait_ge(S["qk_ok"], l * 8 + 2 * hp + 2)
                    for e in (0, 1):
                        q, kt = LNT[e], KT[e]
                        for i, bank, o in ((3, 0, 0), (2, 1, 0), (0, 1, 384), (1, 2, 0)):
                            n = 128 * (i + 1)
                            mm(PS[:, 3 * e + bank, o:o + n], q[:, i * 128:(i + 1) * 128], kt[:, 0:n], True, True)
                        mm(PS[0:NS, 3 * e + 2, 256:416], q[:, NP_:T], kt[:, NP_:NK], True, True).then_inc(S["sc_mm"], 1)
                    for e in (0, 1):
                        h = 2 * hp + e
                        pe.wait_ge(S["p_ok"], l * 8 + h + 1)
                        if e:
                            pe.wait_ge(S["pt_a"], l * 8 + h)
                            pe.wait_ge(S["pt_d"], l * 8 + h)
                        p = P[e]
                        for kb in range(4):
                            for i in range(kb, 4):
                                bank, o = ((6, 0), (7, 0), (3 * e, 0), (7, 384))[kb]
                                po = 128 * (i * (i + 1) // 2 + kb)
                                pe.transpose(PS[:, bank, o + (i - kb) * 128:o + (i - kb + 1) * 128], p[:, po:po + 128], IDENT)
                        pe.transpose(PS[:, 3 * e, 256:288], p[0:NS, 1280:1408], IDENT[0:NS, 0:NS])
                        pe.transpose(PS[0:NS, 3 * e, 288:320], p[0:NS, 1408:1440], IDENT[0:NS, 0:NS]).then_inc(S["pt_mm"], 1)
                        pe.wait_ge(S["pt_a"], l * 8 + h + 1)
                        pe.wait_ge(S["pt_d"], l * 8 + h + 1)
                        r = slice(64 * e, 64 * e + 64)
                        for kb in range(4):
                            po = (0, 512, 896, 1152)[kb]
                            mm(PS[r, 1, kb * 128:512], V[:, kb * 512 + h * 64:kb * 512 + (h + 1) * 64],
                               PT[:, po:po + 512 - 128 * kb], kb == 0, kb == 3)
                        mm(PS[r, 2, 0:NS], V[:, 4 * 512 + h * 64:4 * 512 + (h + 1) * 64], PT[:, 1280:1312], True, False)
                        mm(PS[r, 2, 0:NS], V[0:NS, 5 * 512 + h * 64:5 * 512 + (h + 1) * 64], PT[0:NS, 1312:1344],
                           False, True).then_inc(S["pv_mm"], 1)

                pe.wait_ge(S["pv_lo"], l * 4 + 4)
                cgv = l * PAIRS_L + BASE["gv"]
                for s in (0, 1):
                    for part, W, ready in ((0, WH, hi_ready), (1, WL, lo_ready)):
                        pe.wait_ge(ready[s], cgv + 1 + part)
                        for kk in range(4):
                            k = 4 * s + kk
                            w = W[s][:, kk * 256:(kk + 1) * 256]
                            for t in range(5):
                                out = PS[:, 4 + t // 2, (t % 2) * 256:(t % 2 + 1) * 256]
                                o = k * T + t * 128
                                m = mm(out, XH[:, o:o + 128], w, k == 0 and part == 0 and t % 2 == 0,
                                       k == 7 and part == 1)
                                if part == 0:
                                    m = mm(out, XL[:, o:o + 128], w, False, False)
                    m.then_inc(w_used[s], 1)
                pe.wait_ge(S["kd_ok"], l + 1)
                for i in range(5):
                    n = 128 if i < 4 else NS
                    out = PS[0:n, 7, i * 128:(i + 1) * 128] if i < 4 else PS[0:n, 3, 0:128]
                    m = pe.transpose(out, LNT[3][:, i * 128:i * 128 + n], IDENT)
                m.then_inc(S["kdt_mm"], 1)

                def part_of(s, tiles, c=None, ready=True, done=None):
                    if ready:
                        pe.wait_ge(hi_ready[s], c + 1)
                    for i, outs, first, last in tiles:
                        w = WH[s][:, i * 128:(i + 1) * 128]
                        for out, xh, xl in outs:
                            mm(out, w, xh, first, False)
                        for out, xh, xl in outs:
                            mm(out, w, xl, False, False)
                    if ready:
                        pe.wait_ge(lo_ready[s], c + 2)
                    for i, outs, first, last in tiles:
                        w = WL[s][:, i * 128:(i + 1) * 128]
                        for out, xh, xl in outs:
                            m_ = mm(out, w, xh, False, last)
                    return m_

                def level_products(j, sample):
                    a, b = (LNT[5], LNT[5]) if j < 7 else (GK, GQ)
                    for h in range(4):
                        r = slice(32 * h, 32 * h + 32)
                        if sample:
                            m_ = mm(PS[0:NS, 4 + h, 0:NS], a[r, NP_:T], b[r, NP_:T], True, True)
                        else:
                            for i in range(4):
                                m_ = mm(PS[:, 4 + h, i * 128:(i + 1) * 128], a[r, i * 128:(i + 1) * 128],
                                        b[r, i * 128:(i + 1) * 128], True, True)
                    return m_

                def step(m, j):
                    c = l * PAIRS_L + BASE["ab"] + m
                    n = l * KC + m
                    if j:
                        pe.wait_ge(S["ml_rd"], n)
                    part_of(0, chunk_tiles(0, XH, XL), c).then_inc(S["ga_mm"], 1)
                    if j:
                        pe.wait_ge(S["tb_ok"], n)
                    else:
                        pe.wait_ge(S["kdt_ok"], l + 1)
                    part_of(0, [(8 + k, halves(2, BH, BL, k), k == 0, k == 1) for k in (0, 1)],
                            ready=False).then_inc(S["pl_mm"], 1)
                    pe.wait_ge(S["ta_ok"], n + 1)
                    part_of(0, [(10, halves(0, BH, BL, 2), True, False)], ready=False).then_inc(w_used[0], 1)
                    if j == 0:
                        for i in range(5):
                            nt = 128 if i < 4 else NS
                            m_ = mm(PS[:, 4 + i // 2, (i % 2) * 256:(i % 2 + 1) * 256], KDT[0:nt, i * 128:(i + 1) * 128],
                                    VT[0:nt, i * 256:(i + 1) * 256], i % 2 == 0, True)
                        m_.then_inc(S["ds_mm"], 1)
                    if j >= 2:
                        if j < 7:
                            pe.wait_ge(S["lv_x"], l * 7 + m + 1)
                        pe.wait_ge(S["lv_sel"], n + 1)
                        settle(pe)
                        level_products(j, True).then_inc(S["smp_mm"], 1)
                    pe.wait_ge(S["pl_rd"], n + 1)
                    part_of(1, chunk_tiles(2, XH, XL), c).then_inc(S["gb_mm"], 1)
                    part_of(1, [(8 + i, halves(0, BH, BL, 3 + i), False, i == 2) for i in range(3)],
                            ready=False).then_inc(w_used[1], 1)
                    if j == 0:
                        pe.wait_ge(S["sb_ok"], l + 1)
                    if j < 2:
                        pe.wait_ge(S["lv_x"], l * 7 + m + 1)
                        pe.wait_ge(S["lv_sel"], n + 1)
                    else:
                        pe.wait_ge(S["smp_sel"], l * 6 + m - 1)
                    level_products(j, False).then_inc(S["lv_mm"], 1)

                step(0, 0)
                step(1, 1)
                with pe.Fori(2, 7) as m_:
                    step(m_, 2)
                step(7, 7)

                c0 = l * PAIRS_L + BASE["cg"]

                def gla_tiles(s):
                    return [(8 + k, halves(4 + 2 * s, BH, BL, 6 + k), k == 0, k == 1) for k in (0, 1)]
                pe.wait_ge(S["ml_rd"], (l + 1) * KC)
                part_of(0, chunk_tiles(0, XH, XL), c0)
                pe.wait_ge(S["lv_sel"], l * 8 + 9)
                for g in (0, 1):
                    for i in range(5):
                        n = 128 if i < 4 else NS
                        bank, o = (4 + g, i * 128) if i < 4 else (6 + g, 0)
                        sb = i - 1 if i < 4 else 4
                        if i > 0:
                            mm(PS[:, bank, o:o + n], SB[:, sb * 256 + g * 128:sb * 256 + (g + 1) * 128],
                               LNT[2][:, i * 128:i * 128 + n], True, False)
                        for e in (0, 1):
                            h = 2 * g + e
                            a = A[:, h * NP_ + i * 128:h * NP_ + (i + 1) * 128] if i < 4 else AS[0:NS, h * NS:(h + 1) * NS]
                            m = mm(PS[64 * e:64 * e + 64, bank, o:o + n], VT[0:n, i * 256 + h * 64:i * 256 + (h + 1) * 64],
                                   a, i == 0, True)
                m.then_inc(S["o_mm"], 1)
                pe.wait_ge(S["tb_ok"], (l + 1) * KC)
                part_of(1, chunk_tiles(2, XH, XL), c0)
                pe.wait_ge(S["o_sq"], l + 1)
                for g in (0, 1):
                    for h in (0, 1):
                        m = mm(PS[:, 4 + 2 * g + h, 0:TH], BLK, LN_[:, g * T + h * TH:g * T + (h + 1) * TH], True, True)
                m.then_inc(S["o_ms"], 1)
                pe.wait_ge(S["o_lo"], l + 1)
                for s in (0, 1):
                    part_of(s, gla_tiles(s), ready=False).then_inc(w_used[s], 1)
                settle(pe)
                with pe.Fori(1, PAIRS["cg"]) as p:
                    for s in (0, 1):
                        pe.wait_ge(bank_free[s], l * USES_L + UBASE["cg"] + p + 1)
                        gemm(s, c0 + p, chunk_tiles(2 * s, XH, XL) + gla_tiles(s))
                first_pair(l, "wo", l, "mx_lo", MXH, MXL)
                standard(l, "wo", MXH, MXL, 1)
                ln_stats(l, 1)

                pe.wait_ge(S["mem_ready"], l + 1)
                settle(pe)
                with pe.Fori(0, PAIRS["memk"]) as p:
                    for s in (0, 1):
                        pe.wait_ge(bank_free[s], l * USES_L + UBASE["memk"] + p + 1)
                        gemm(s, l * PAIRS_L + BASE["memk"] + p,
                             [(k, [(PS[:, 2 * s, 0:NMEM], MMH[:, k * NMEM:(k + 1) * NMEM],
                                    MML[:, k * NMEM:(k + 1) * NMEM])], k == 0, k == KC - 1) for k in range(KC)])
                with pe.Fori(0, 2) as q:
                    for u in (0, 1):
                        pe.wait_ge(bank_free[u], l * USES_L + UBASE["memv"] + q + 1)
                        for s in (0, 1):
                            c = l * PAIRS_L + BASE["memv"] + q * 2 + u
                            kk0 = 4 * s
                            pe.wait_ge(hi_ready[s], c + 1)
                            for kk in range(4):
                                w = WH[s][:, kk * 256:(kk + 1) * 256]
                                for t in (0, 1):
                                    o = (kk0 + kk) * NMEM + t * 128
                                    out = PS[:, 2 * u, t * 256:(t + 1) * 256]
                                    mm(out, MMH[:, o:o + 128], w, kk0 + kk == 0 and t == 0, False)
                                    mm(out, MML[:, o:o + 128], w, False, False)
                            pe.wait_ge(lo_ready[s], c + 2)
                            for kk in range(4):
                                w = WL[s][:, kk * 256:(kk + 1) * 256]
                                for t in (0, 1):
                                    o = (kk0 + kk) * NMEM + t * 128
                                    out = PS[:, 2 * u, t * 256:(t + 1) * 256]
                                    m = mm(out, MMH[:, o:o + 128], w, False, kk0 + kk == 7)
                            m.then_inc(w_used[s], 1)

                pe.wait_ge(S["cmem_in"], (l + 1) * 32)
                first_pair(l, "cq", 4 * l + 2)
                free = l * USES_L + UBASE["cq"]
                for h in range(4):
                    for s in (0, 1):
                        pe.wait_ge(bank_free[s], free + h + 2)
                    for i in range(4):
                        for c in (0, 1):
                            mm(PS[:, 4 + i // 2, (i % 2) * 256:(i % 2 + 1) * 256], LNT[c][:, i * 128:(i + 1) * 128],
                               MK[0][:, (2 * h + c) * NMEM:(2 * h + c + 1) * NMEM], c == 0, c == 1)
                    for c in (0, 1):
                        m = mm(PS[0:NS, 6, 0:NMEM], LNT[c][:, NP_:T], MK[1][:, (2 * h + c) * NMEM:(2 * h + c + 1) * NMEM],
                               c == 0, c == 1)
                    m.then_inc(S["csc_mm"], 1)
                    if h:
                        pe.wait_ge(S["cpv_lo"], l * 8 + 2 * h)
                    if h < 3:
                        gemm(0, l * PAIRS_L + BASE["cq"] + h + 1, chunk_tiles(0, XH, XL))
                    pe.wait_ge(S["cp_ok"], l * 4 + h + 1)
                    p = CP[h % 2]
                    for kb in (0, 1):
                        for i in range(4):
                            pe.transpose(PS[:, (7, 4)[kb], i * 128:(i + 1) * 128],
                                         p[:, i * 256 + kb * 128:i * 256 + (kb + 1) * 128], IDENT)
                    for kb in (0, 1):
                        m = pe.transpose(PS[:, 6, kb * NS:(kb + 1) * NS], p[0:NS, 1024 + kb * 128:1024 + (kb + 1) * 128],
                                         IDENT[0:NS, 0:NS])
                    m.then_inc(S["cpt_mm"], 1)
                    if h < 3:
                        gemm(1, l * PAIRS_L + BASE["cq"] + h + 1, chunk_tiles(2, XH, XL))
                        pe.wait_ge(bank_free[0], free + h + 3)
                    pe.wait_ge(S["cpt_d"], l * 4 + h + 1)
                    bp, bs = CPV[h]
                    for c in (0, 1):
                        d0 = h * 256 + c * 128
                        for kb in (0, 1):
                            mm(PS[:, bs, c * NS:(c + 1) * NS], MV[1][:, kb * D + d0:kb * D + d0 + 128],
                               CPT[:, kb * T + NP_:(kb + 1) * T], kb == 0, kb == 1)
                    for c in (0, 1):
                        d0 = h * 256 + c * 128
                        for kb in (0, 1):
                            m = mm(PS[:, bp[c], 0:NP_], MV[0][:, kb * D + d0:kb * D + d0 + 128],
                                   CPT[:, kb * T:kb * T + NP_], kb == 0, kb == 1)
                        m.then_inc(S["cpv_mm"], 1)
                first_pair(l, "co", l, "cpv_lo", OH, OL)
                standard(l, "co", OH, OL, 1)
                ln_stats(l, 2)

                first_pair(l, "f2i", 4 * l + 3)
                standard(l, "f2i", XH, XL, 1)
                ffn_out(l, "f2o", l * 2 + 1)
                ln_stats(l, 3)

        @block.scalar
        def _(act):
            def f(out, in_, func, **kw):
                return act.activation(out, in_, func, **kw)

            def load(dst, src, s):
                return act.dma_start(dst, src).then_inc(S[s], 16)

            def convert(s, tiles, c):
                act.wait_ge(landed[s], (c + 1) * 16)
                act.wait_ge(w_used[s], c + 1)
                n = tiles * 128
                f(WH[s][:, 0:n], WR[s][:, 0:n], ACT.Copy).then_inc(hi_ready[s], 1)

            def pair(l, name, p, s, last):
                c = l * PAIRS_L + BASE[name] + p + 1
                if not last:
                    convert(s, TILES[name], c)
                else:
                    convert(s, TILES[NEXT[name]], c)

            def phase(l, name, body=None, unroll=1):
                n = PAIRS[name]
                if n > unroll:
                    with act.Fori(0, n // unroll - 1) as q:
                        for u in range(unroll):
                            for s in (0, 1):
                                pair(l, name, q * unroll + u, s, False)
                                if body:
                                    body(q * unroll + u, u, s, q)
                for u in range(unroll):
                    for s in (0, 1):
                        pair(l, name, n - unroll + u, s, u == unroll - 1)
                        if body:
                            body(n - unroll + u, u, s, n // unroll - 1)

            def square(n, m, b):
                act.wait_ge(S["y_upd"], n * KC + m + 1)
                act.wait_ge(S["q_add"], n * KC + m + 1)
                f(SQ[b], Yf[:, bass.ds(m * T, T)], ACT.Square).then_inc(S["y_sq"], 1)

            def ln_mean(n):
                act.wait_ge(S["stats_mm"], n + 1)
                f(two(MEAN), banks2(4), ACT.Copy, scale=1.0 / D).then_inc(S["mean"], 1)

            def ln_rstd(n):
                act.wait_ge(S["var"], n + 1)
                f(RSTD, RSTD, ACT.Ln)
                act.drain()
                f(RSTD, RSTD, ACT.Exp, scale=-0.5).then_inc(S["rstd"], 1)

            def ln_chunk(n, j, c):
                act.wait_ge(S["ln_d"], n * KC + c + 1)
                f(Y[:, c, :], Y[:, c, :], ACT.Identity, scale=SMALL[:, SM_LNG + j * KC + c:SM_LNG + j * KC + c + 1],
                  bias=SMALL[:, SM_LNB + j * KC + c:SM_LNB + j * KC + c + 1])
                act.drain()
                f(XH[:, c * T:(c + 1) * T], Y[:, c, :], ACT.Copy).then_inc(S["x_hi"], 1)

            def layer_norm(n, j):
                ln_mean(n)
                ln_rstd(n)
                for c in range(KC):
                    ln_chunk(n, j, c)

            for i in range(4):
                part = slice(i * 2 * T, (i + 1) * 2 * T)
                load(Yf[:, part], io["x"][:, part], f"x_in{i}")
            load(TAB[:, :], io["tab"], "const_in")
            load(CST[:, :], io["cst"], "const_in")
            load(LN_[:, 0:1024], io["mask"], "const_in")
            for s in (0, 1):
                convert(s, TILES["f1i"], 0)
            for c in range(KC):
                if c % 2 == 0:
                    act.wait_ge(S[f"x_in{c // 2}"], 16)
                f(XH[:, c * T:(c + 1) * T], Y[:, c, :], ACT.Copy).then_inc(S["x_hi"], 1)

            with act.Fori(0, L) as l:
                act.wait_ge(S["x_ready"], (4 * l + 1) * KC)
                load(SMALL[:, :], io["small"][l], "small_in")
                act.wait_ge(S["small_in"], (l + 1) * 16)

                def ffn_in(l, name):
                    def body(p, u, s, q):
                        if s == 0:
                            act.wait_ge(w_used[0], l * PAIRS_L + BASE[name] + p + 2)
                            act.wait_ge(bank_free[1], l * USES_L + UBASE[name] + p + 1)
                            f(two(LNT[2]), banks2(0), ACT.Silu).then_inc(bank_free[0], 1)
                    phase(l, name, body)

                def ffn_out(l, name, n):
                    phase(l, name, lambda p, u, s, q: square(n, p, u) if s else None, 2)

                ffn_in(l, "f1i")
                ffn_out(l, "f1o", 4 * l)
                act.wait_ge(S["stats_mm"], 4 * l + 1)
                for c in (0, 1):
                    load(U[:, c * UW + UQ:c * UW + UQ + HIST], io["pool_in"][l][:, c * HIST:(c + 1) * HIST], "hist_in")
                    load(CK[:, c * NK + T:(c + 1) * NK], io["ckv_in"][l][:, c * PAST:(c + 1) * PAST], "caches_in")
                for r in (64, 96):
                    load(KR[r:r + 32, T:NK], io["krope_in"][l], "caches_in")
                layer_norm(4 * l, 0)

                def mean_square(i, src):
                    w = (T, NK)[i]
                    f(LN_[:, 0:2 * T].rearrange("p (c t) -> p c t", c=2),
                      src[:, :].rearrange("p (c t) -> p c t", c=2)[:, :, 0:T], ACT.Square).then_inc(S["rq_sq"], 1)

                def root(i):
                    act.wait_ge(S["rq_v"], 2 * l + i + 1)
                    f(LNT[2], LNT[2], ACT.Ln)
                    act.drain()
                    f(LNT[2], LNT[2], ACT.Exp, scale=-0.5).then_inc(S["rq_r"], 1)

                for p in range(3):
                    for s in (0, 1):
                        pair(l, "win", p, s, False)
                act.wait_ge(S["pooled"], l + 1)
                mean_square(0, QL)
                for c in (0, 1):
                    act.dma_start(io["pool_p"][l][:, c * HIST:(c + 1) * HIST],
                                  U[:, c * UW + NP_:c * UW + NP_ + HIST]).then_inc(S["st_pool"], 16)
                    act.dma_start(io["pool_s"][l][:, c * HIST:(c + 1) * HIST],
                                  U[:, (c + 1) * UW - HIST:(c + 1) * UW]).then_inc(S["st_pool"], 16)
                for s in (0, 1):
                    pair(l, "win", 3, s, False)
                act.wait_ge(S["z_mm"], l + 1)
                act.wait_ge(S["kr_ready"], l + 1)
                f(two(LNT[4]), banks2(4), ACT.Abs, bias=SMALL[:, SM_BA:SM_BA + 1]).then_inc(S["z_abs"], 1)
                act.drain()
                f(LNT[4], LNT[4], ACT.Exp, scale=-1.0)
                act.drain()
                f(LNT[4], LNT[4], ACT.Ln, bias=1.0).then_inc(S["z_l"], 1)
                act.dma_start(io["krope"][l], KR[64:96, 0:T]).then_inc(S["st_kr"], 16)
                root(0)
                act.wait_ge(S["rq_mm"], 2 * l + 1)
                mean_square(1, CK)
                for s in (0, 1):
                    pair(l, "win", 4, s, False)
                root(1)

                def pool_hi(c):
                    act.wait_ge(S["pool_mm"], 2 * l + c + 1)
                    f(two(BH[:, c * T:(c + 1) * T]), banks2(4), ACT.Copy,
                      scale=SMALL[:, SM_PS + c:SM_PS + c + 1]).then_inc(S["pool_hi"], 1)
                pool_hi(0)
                act.wait_ge(S["ck_in"], 2 * l + 2)
                for c in (0, 1):
                    act.dma_start(io["ckv"][l][:, c * T:(c + 1) * T], CK[:, c * NK:c * NK + T]).then_inc(S["st_ck"], 16)
                act.wait_ge(S["caches_in"], (l + 1) * 64)
                f(QH[:, :], QL[:, :], ACT.Copy).then_inc(S["latr_hi"], 1)
                f(CH[:, 0:2 * NK], CK[:, :], ACT.Copy).then_inc(S["latr_hi"], 1)
                for s in (0, 1):
                    pair(l, "win", 5, s, True)
                    f(two(LNT[s]), banks2(2 * s), ACT.Tanh, scale=0.5).then_inc(S["tanh_r"], 1)
                pool_hi(1)
                act.wait_ge(S["st_pool"], (l + 1) * 64)
                act.wait_ge(S["st_ck"], (l + 1) * 32)
                for s in (0, 1):
                    pair(l, "vup", 0, s, True)
                act.wait_ge(w_used[1], l * PAIRS_L + BASE["vup"] + 2)
                f(V[:, 4 * 512:5 * 512], PS[:, 4, 0:512], ACT.Copy)
                f(V[0:NS, 5 * 512:6 * 512], PS[0:NS, 5, 0:512], ACT.Copy).then_inc(S["v_ok"], 1)
                for hp in range(4):
                    s = hp % 2
                    act.wait_ge(w_used[s], l * PAIRS_L + BASE["mla"] + hp // 2 + 2)
                    for e in (0, 1):
                        i = f(two(KT[e][0:64, :]), PS[64 * e:64 * e + 64, 4:6, 0:KH], ACT.Copy)
                    i.then_inc(S["qk_ok"], 1)
                    pair(l, "mla", hp // 2, s, hp >= 2)
                    for e in (0, 1):
                        h = 2 * hp + e
                        act.wait_ge(S["mx_ok"], l * 8 + h + 1)
                        c0 = 16 * e
                        for i, bank, o in ((3, 0, 0), (2, 1, 0), (0, 1, 384), (1, 2, 0)):
                            for hf in (0, 1):
                                r = slice(64 * hf, 64 * hf + 64)
                                n = 128 * i + 64 * (hf + 1)
                                po = 128 * (i * (i + 1) // 2)
                                f(P[e][r, po:po + n], PS[r, 3 * e + bank, o:o + n], ACT.Exp, scale=MLA_SCALE,
                                  bias=SC[r, c0 + 5 + i:c0 + 6 + i], accum_out=SC[r, c0 + 10 + i:c0 + 11 + i])
                        f(P[e][0:NS, 1280:1440], PS[0:NS, 3 * e + 2, 256:416], ACT.Exp, scale=MLA_SCALE,
                          bias=SC[0:NS, c0 + 9:c0 + 10], accum_out=SC[0:NS, c0 + 14:c0 + 15])
                        act.drain().then_inc(S["exp_ok"], 1)
                    for e in (0, 1):
                        h = 2 * hp + e
                        act.wait_ge(S["pt_mm"], l * 8 + h + 1)
                        if e:
                            act.wait_ge(S["pv_mm"], l * 8 + h)
                        f(PT[:, 896:1152], PS[:, 3 * e, 0:256], ACT.Copy)
                        f(PT[:, 1280:1312], PS[:, 3 * e, 256:288], ACT.Copy)
                        f(PT[0:NS, 1312:1344], PS[0:NS, 3 * e, 288:320], ACT.Copy).then_inc(S["pt_a"], 1)
                    act.wait_ge(S["pv_mm"], l * 8 + 2 * hp + 2)
                    o = (2 + hp) * T
                    f(BH[:, o:o + NP_], PS[:, 1, 0:NP_], ACT.Copy)
                    f(BH[:, o + NP_:o + T], PS[:, 2, 0:NS], ACT.Copy).then_inc(S["pv_hi"], 1)

                for s in (0, 1):
                    pair(l, "gv", 0, s, True)
                    if s == 0:
                        f(LNT[1], B, ACT.Exp, scale=1.0 / 16).then_inc(S["eb_ok"], 1)
                        act.wait_ge(S["kd_sub"], l + 1)
                        f(LNT[3], LNT[3], ACT.Exp, scale=1.0 / 16).then_inc(S["kdE"], 1)
                        act.wait_ge(S["z_in"], l + 1)
                        for h in range(4):
                            r = slice(32 * h, 32 * h + 32)
                            load(SB[r, 4 * 256 + h * 64:4 * 256 + (h + 1) * 64], io["gla_in"][l][r, :], "gla_in")

                def level_exp(j, w):
                    act.wait_ge(S["lv_e"], l * 7 + j + 1)
                    f(LNT[4][:, 0:w], LNT[4][:, 0:w], ACT.Exp, scale=1.0 / 16).then_inc(S["lv_E"], 1)
                level_exp(0, NP_)

                def step(m, w, last=False):
                    n = l * KC + m
                    if w:
                        level_exp(m + 1, w)
                    act.wait_ge(S["ga_mm"], n + 1)
                    if not (isinstance(m, int) and m == 0):
                        act.wait_ge(S["pl_rd"], n)
                    f(two(LNT[0]), banks2(0), ACT.Tanh, scale=0.5).then_inc(S["ta_ok"], 1)
                    pair(l, "ab", m, 0, last)
                    act.wait_ge(S["gb_mm"], n + 1)
                    if isinstance(m, int) and m == 0:
                        act.wait_ge(S["sb_ok"], l + 1)
                        for h in range(4):
                            r = slice(32 * h, 32 * h + 32)
                            for sb, dst in ((3, "gla_p"), (5, "gla_s")):
                                act.dma_start(io[dst][l][r, :], SB[r, sb * 256 + h * 64:sb * 256 + (h + 1) * 64]).then_inc(
                                    S["st_gla"], 16)
                    else:
                        act.wait_ge(S["ml_rd"], n)
                    f(two(LNT[1]), banks2(2), ACT.Tanh, scale=0.5).then_inc(S["tb_ok"], 1)
                    pair(l, "ab", m, 1, last)
                step(0, NP_)
                with act.Fori(1, 6) as m:
                    step(m, T)
                step(6, 0)
                step(7, 0, True)
                act.wait_ge(S["o_ok"], l + 1)
                f(LN_[:, 0:2 * T], O[:, :], ACT.Square).then_inc(S["o_sq"], 1)
                act.wait_ge(S["o_v"], l + 1)
                f(LN_[:, 2 * T:4 * T], LN_[:, 2 * T:4 * T], ACT.Ln)
                act.drain()
                f(LN_[:, 2 * T:4 * T], LN_[:, 2 * T:4 * T], ACT.Exp, scale=-0.5).then_inc(S["o_r"], 1)
                act.wait_ge(S["o_y"], l + 1)
                f(BH[:, 6 * T:8 * T], O[:, :], ACT.Copy).then_inc(S["o_hi"], 1)
                act.wait_ge(S["o_lo"], l + 1)
                act.wait_ge(S["st_gla"], (l + 1) * 128)
                load(MRAW[:, :], io["mem"], "mem_in")

                def cg(p, u, s, q):
                    m = p * 2 + s
                    act.wait_ge(w_used[s], l * PAIRS_L + BASE["cg"] + p + 2)
                    f(two(LNT[4 + s]), banks2(2 * s), ACT.Tanh, scale=0.5).then_inc(S["tc_ok"], 1)
                    act.wait_ge(S["m_ok"], l * KC + m + 1)
                    f(MXH[:, bass.ds(m * T, T)], LNT[s], ACT.Copy, scale=0.5).then_inc(S["mx_hi"], 1)
                phase(l, "cg", cg)
                for s in (0, 1):
                    act.wait_ge(w_used[s], l * PAIRS_L + BASE["wo"] + 1)
                load(MK[1][:, :], io["memk_in"][l], "cmem_in")
                load(MV[1][:, :], io["memv_in"][l], "cmem_in")
                act.wait_ge(S["mem_in"], (l + 1) * 16)
                f(MMH[:, :], MRAW[:, :], ACT.Copy).then_inc(S["mem_hi"], 1)
                phase(l, "wo", lambda p, u, s, q: square(4 * l + 1, p * 2 + s, s))
                n = 4 * l + 1
                ln_mean(n)
                for i, (name, p) in enumerate([(m, p) for m in ("memk", "memv") for p in range(4)]):
                    for s in (0, 1):
                        pair(l, name, p, s, p == 3)
                    if i == 0:
                        ln_rstd(n)
                    elif i < 5:
                        for c in (2 * i - 2, 2 * i - 1):
                            ln_chunk(n, 1, c)
                for s in (0, 1):
                    act.wait_ge(bank_free[s], l * USES_L + UBASE["memv"] + 3)
                act.dma_start(io["mem_k"][l], MK[0][:, :]).then_inc(S["st_mem"], 16)
                act.dma_start(io["mem_v"][l], MV[0][:, :]).then_inc(S["st_mem"], 16)

                for s in (0, 1):
                    pair(l, "cq", 0, s, False)
                for h in range(4):
                    act.wait_ge(S["cmx_ok"], l * 4 + h + 1)
                    c0 = 16 * (h % 2)
                    for i in range(4):
                        f(CP[h % 2][:, i * 256:(i + 1) * 256], PS[:, 4 + i // 2, (i % 2) * 256:(i % 2 + 1) * 256], ACT.Exp,
                          scale=MEM_SCALE, bias=SC[:, c0 + 5 + i:c0 + 6 + i], accum_out=SC[:, c0 + 10 + i:c0 + 11 + i])
                    f(CP[h % 2][0:NS, 1024:1280], PS[0:NS, 6, 0:256], ACT.Exp, scale=MEM_SCALE,
                      bias=SC[0:NS, c0 + 9:c0 + 10], accum_out=SC[0:NS, c0 + 14:c0 + 15])
                    act.drain().then_inc(S["cexp_ok"], 1)
                    if h < 3:
                        for s in (0, 1):
                            pair(l, "cq", h + 1, s, h == 2)
                    for c in (0, 1):
                        act.wait_ge(S["cpv_mm"], l * 8 + 2 * h + c + 1)
                        o = (2 * h + c) * T
                        bp, bs = CPV[h]
                        if c == 0:
                            f(OH[:, o:o + 2 * T].rearrange("p (c t) -> p c t", c=2)[:, :, NP_:T],
                              PS[:, bs, 0:2 * NS].rearrange("p (c t) -> p c t", c=2), ACT.Copy)
                        f(OH[:, o:o + NP_], PS[:, bp[c], 0:NP_], ACT.Copy).then_inc(S["cpv_hi"], 1)
                phase(l, "co", lambda p, u, s, q: square(4 * l + 2, p * 2 + s, s))
                layer_norm(4 * l + 2, 2)
                ffn_in(l, "f2i")
                ffn_out(l, "f2o", 4 * l + 3)
                layer_norm(4 * l + 3, 3)
            act.wait_ge(S["x_ready"], (4 * L + 1) * KC)
            act.dma_start(io["y"], Yf[:, :]).then_inc(S["st_y"], 16)
            act.wait_ge(S["st_y"], 16)

        @block.vector
        def _(ve):
            def tt(out, a, b, op):
                return ve.tensor_tensor(out, a, b, op)

            def stt(out, a, sc, b, op0, op1):
                return ve.scalar_tensor_tensor(out, a, sc, b, op0, op1)

            def group_done(l, name, p, s):
                ve.wait_ge(w_used[s], l * PAIRS_L + BASE[name] + p + 2)

            def residual(n, m, b, scale):
                y = Yf[:, bass.ds(m * T, T)]
                stt(two(y), banks2(2 * b), scale, two(y), ALU.mult, ALU.add).then_inc(bank_free[b], 1)
                ve.drain().then_inc(S["y_upd"], 1)
                tt(YS, YS, y, ALU.add)
                ve.wait_ge(S["y_sq"], n * KC + m + 1)
                tt(QS, QS, SQ[b], ALU.add).then_inc(S["q_add"], 1)

            def clear_sums():
                ve.drain()
                ve.memset(YS, 0.0)
                ve.memset(QS, 0.0)
                ve.drain()

            def ln_var(n):
                ve.drain().then_inc(S["stats_ready"], 1)
                ve.wait_ge(S["mean"], n + 1)
                tt(LNT[5], MEAN, MEAN, ALU.mult)
                ve.drain()
                stt(two(RSTD), banks2(6), 1.0 / D, two(LNT[5]), ALU.mult, ALU.subtract)
                ve.drain()
                ve.tensor_scalar(RSTD, RSTD, 0.0, EPS / ALPHA ** 2, ALU.max, ALU.add).then_inc(S["var"], 1)

            def ln_chunk(c):
                y = Yf[:, bass.ds(c * T, T)]
                tt(y, y, MEAN, ALU.subtract)
                ve.drain()
                tt(y, y, RSTD, ALU.mult).then_inc(S["ln_d"], 1)

            def layer_norm(n):
                ln_var(n)
                ve.wait_ge(S["rstd"], n + 1)
                settle(ve)
                with ve.Fori(0, KC) as c:
                    ln_chunk(c)

            ve.memset(XH[:, KC * T:].bitcast(F32), 0.0)
            ve.memset(XL[:, KC * T:].bitcast(F32), 0.0)
            ve.memset(SC[:, :], 1.0)
            for s in (0, 1):
                ve.sem_inc(bank_free[s], 1)
            ve.sem_inc(S["lv_sel"], 1)
            ve.sem_inc(S["q_add"], 2)
            ve.wait_ge(S["const_in"], 16 * 3)
            ve.tensor_copy(MASK[:, :], LN_[:, 0:1024])
            ve.drain()

            with ve.Fori(0, L) as l:
                ve.wait_ge(S["small_in"], (l + 1) * 16)
                settle(ve)
                def ffn_in(l, name):
                    with ve.Fori(0, FC) as p:
                        ve.wait_ge(bank_free[0], l * USES_L + UBASE[name] + p + 2)
                        group_done(l, name, p, 1)
                        h = bass.ds(p * T, T)
                        settle(ve)
                        ve.drain()
                        tt(two(LNT[3]), two(LNT[2]), banks2(2), ALU.mult).then_inc(bank_free[1], 1)
                        ve.drain()
                        ve.tensor_copy(HH[:, h], LNT[3])
                        ve.drain()
                        tt(HL[:, h], LNT[3], HH[:, h].bitcast(F32), ALU.subtract).then_inc(S["h_ready"], 1)

                def ffn_out(l, name, n):
                    clear_sums()
                    with ve.Fori(0, 4) as q:
                        for u in (0, 1):
                            group_done(l, name, q * 2 + u, 1)
                            residual(n, q * 2 + u, u, 0.5 / ALPHA)
                    layer_norm(n)

                def proj_out(l, name, n):
                    clear_sums()
                    with ve.Fori(0, 4) as p:
                        for s in (0, 1):
                            group_done(l, name, p, s)
                            residual(n, p * 2 + s, s, 1.0 / ALPHA)

                ffn_in(l, "f1i")
                clear_sums()
                with ve.Fori(0, 4) as q:
                    for u in (0, 1):
                        group_done(l, "f1o", q * 2 + u, 1)
                        residual(4 * l, q * 2 + u, u, 0.5 / ALPHA)
                layer_norm(4 * l)
                for c in (0, 1):
                    ve.memset(U[:, c * UW:c * UW + HIST], 0.0)

                def group(g):
                    p, s = g // 2, g % 2
                    group_done(l, "win", p, s)
                    src = banks2(2 * s)
                    if g < 2:
                        o = g * UW
                        ve.tensor_copy(U[:, o + HIST:o + HIST + TH], PS[:, 2 * s, 0:TH])
                        ve.tensor_copy(U[:, o + HIST + TH:o + HIST + NP_], PS[:, 2 * s + 1, 0:NP_ - TH])
                        i = ve.tensor_copy(U[:, o + UQ + HIST:o + UW], PS[:, 2 * s + 1, NP_ - TH:TH])
                    elif g < 4:
                        i = ve.tensor_copy(two(QL[:, s * T:(s + 1) * T]), src)
                    elif g < 6:
                        i = ve.tensor_copy(two(CK[:, s * NK:s * NK + T]), src)
                    elif g == 6:
                        ve.tensor_copy(two(GA[0:16, :]), PS[0:16, 0:2, 0:TH])
                        i = tt(two(LNT[4][64:128, :]), PS[64:128, 0:2, 0:TH], two(KCOS[64:128, :]), ALU.mult)
                    elif g == 7:
                        i = tt(two(LNT[5][64:128, :]), PS[64:128, 2:4, 0:TH], two(KSIN[64:128, :]), ALU.mult)
                        i.then_inc(bank_free[s], 1)
                        ve.drain()
                        tt(KR[64:128, 0:T], LNT[4][64:128, :], LNT[5][64:128, :], ALU.add).then_inc(S["kr_ready"], 1)
                        return
                    elif g == 8:
                        i = ve.tensor_scalar(two(GQ[:, :]), src, 32.0 ** -0.5, None, ALU.mult)
                    elif g == 9:
                        i = ve.tensor_copy(two(GK[:, :]), src)
                    else:
                        ve.wait_ge(S["tanh_r"], l * 2 + s + 1)
                        i = stt(two(SG[:, s * T:(s + 1) * T]), two(LNT[s]), 1.0, src, ALU.add, ALU.mult)
                    i.then_inc(bank_free[s], 1)

                for g in range(4):
                    group(g)
                ve.wait_ge(S["hist_in"], (l + 1) * 32)
                settle(ve)
                ve.drain()
                U3 = U[:, :].rearrange("p (c t) -> p c t", c=2)
                W1 = LN_[:, 0:2 * UW].rearrange("p (c t) -> p c t", c=2)
                W2 = LN_[:, 2 * UW:4 * UW].rearrange("p (c t) -> p c t", c=2)
                O3 = UP[:, :].rearrange("p (c t) -> p c t", c=2)
                tt(W1[:, :, 1:], U3[:, :, 1:], U3[:, :, :UW - 1], ALU.add)
                ve.drain()
                tt(W2[:, :, 3:], W1[:, :, 3:], W1[:, :, 1:UW - 2], ALU.add)
                ve.drain()
                tt(W1[:, 1, 7:], W2[:, 1, 7:], W2[:, 1, 3:UW - 4], ALU.add)
                ve.drain()
                tt(W2[64:128, 1, 15:], W1[64:128, 1, 15:], W1[64:128, 1, 7:UW - 8], ALU.add)
                ve.drain()
                for g in (4, 5):
                    group(g)
                for r, W in ((slice(0, 64), W1), (slice(64, 128), W2)):
                    for c in (0, 1):
                        for o, u0, n in ((0, HIST, NP_), (NP_, UQ + HIST, NS)):
                            stt(O3[r, c, o:o + n], W[r, c, u0:u0 + n], INVW[r, c:c + 1], U3[r, c, u0:u0 + n],
                                ALU.mult, ALU.subtract)
                ve.drain()
                for r, W in ((slice(0, 64), W1), (slice(64, 128), W2)):
                    tt(O3[r, :, 0:16], W[r, :, HIST:HIST + 16], INVC[r, :, :], ALU.mult)
                ve.drain()
                for r in (slice(0, 64), slice(64, 128)):
                    tt(O3[r, :, 0:16], O3[r, :, 0:16], U3[r, :, HIST:HIST + 16], ALU.subtract)
                ve.drain().then_inc(S["pooled"], 1)
                for g in (6, 7):
                    group(g)

                def latent(i, buf, w, g0):
                    ve.drain()
                    ve.wait_ge(S["rq_mm"], 2 * l + i + 1)
                    ve.tensor_scalar(two(LNT[2]), banks2(6), 1.0 / 256, EPS, ALU.mult, ALU.add).then_inc(S["rq_v"], 1)
                    ve.wait_ge(S["rq_r"], 2 * l + i + 1)
                    for c in (0, 1):
                        b = buf[:, c * w:c * w + T]
                        j = stt(b, b, SMALL[:, g0 + c:g0 + c + 1], LNT[2], ALU.mult, ALU.mult)
                    j.then_inc(S["ck_in"], 1)

                ve.wait_ge(S["z_abs"], l + 1)
                ve.tensor_scalar(two(LNT[5]), banks2(4), SMALL[:, SM_BA:SM_BA + 1], 0.0, ALU.add, ALU.min)
                ve.wait_ge(S["z_l"], l + 1)
                settle(ve)
                ve.drain()
                tt(LNT[3], LNT[5], LNT[4], ALU.subtract)
                ve.drain()
                ve.tensor_tensor_scan(B, RESET, LNT[3], 0.0, ALU.mult, ALU.add).then_inc(S["B_ok"], 1)
                latent(0, QL, T, SM_QN)
                for g in (8, 9):
                    group(g)
                latent(1, CK, NK, SM_KN)

                def pool_out(c):
                    ve.wait_ge(S["pool_hi"], l * 2 + c + 1)
                    stt(two(BL[:, c * T:(c + 1) * T]), banks2(4), SMALL[:, SM_PS + c:SM_PS + c + 1],
                        two(BH[:, c * T:(c + 1) * T].bitcast(F32)), ALU.mult, ALU.subtract).then_inc(S["pool_lo"], 1)
                pool_out(0)
                ve.wait_ge(S["latr_hi"], l * 2 + 1)
                tt(QO[:, :], QL[:, :], QH[:, :].bitcast(F32), ALU.subtract)
                ve.wait_ge(S["latr_hi"], l * 2 + 2)
                tt(CO[:, 0:2 * NK], CK[:, :], CH[:, 0:2 * NK].bitcast(F32), ALU.subtract)
                ve.memset(CH[:, 2 * NK:].bitcast(F32), 0.0)
                ve.memset(CO[:, 2 * NK:].bitcast(F32), 0.0)
                ve.drain().then_inc(S["lat_ready"], 1)
                for g in (10, 11):
                    group(g)
                pool_out(1)
                ve.wait_ge(S["st_ck"], (l + 1) * 32)
                settle(ve)
                ve.drain()
                for e in (0, 1):
                    ve.memset(P[e][:, 0:1280], 0.0)
                    ve.tensor_copy(KT[e][64:128, :], KR[64:128, :])
                group_done(l, "vup", 0, 1)
                ve.tensor_copy(V[:, 0:2048].rearrange("p (b t) -> p b t", b=4), PS[:, 0:4, :]).then_inc(S["v_ok"], 1)
                for hp in range(4):
                    s = hp % 2
                    group_done(l, "mla", hp // 2, s)
                    for e in (0, 1):
                        j = tt(two(LNT[e]), banks2(2 * e), two(QTAB), ALU.mult)
                    j.then_inc(S["qk_ok"], 1)
                    for e in (0, 1):
                        h = 2 * hp + e
                        c0 = 16 * e
                        ve.wait_ge(S["sc_mm"], l * 8 + h + 1)
                        for i, bank, o in ((3, 0, 0), (2, 1, 0), (0, 1, 384), (1, 2, 0)):
                            for hf in (0, 1):
                                r = slice(64 * hf, 64 * hf + 64)
                                ve.reduce_max(SC[r, c0 + i:c0 + i + 1], PS[r, 3 * e + bank, o:o + 128 * i + 64 * (hf + 1)], AX.X)
                        ve.reduce_max(SC[0:NS, c0 + 4:c0 + 5], PS[0:NS, 3 * e + 2, 256:416], AX.X)
                        ve.drain()
                        ve.tensor_scalar(SC[:, c0 + 5:c0 + 10], SC[:, c0:c0 + 5], -MLA_SCALE, None, ALU.mult).then_inc(S["mx_ok"], 1)
                    for e in (0, 1):
                        h = 2 * hp + e
                        c0 = 16 * e
                        ve.wait_ge(S["exp_ok"], l * 8 + h + 1)
                        ve.reciprocal(SC[:, c0 + 10:c0 + 15], SC[:, c0 + 10:c0 + 15])
                        ve.drain()
                        for i in range(4):
                            po = 128 * (i * (i + 1) // 2)
                            b = P[e][:, po:po + 128 * (i + 1)]
                            ve.tensor_scalar(b, b, SC[:, c0 + 10 + i:c0 + 11 + i], None, ALU.mult)
                        b = P[e][0:NS, 1280:1440]
                        ve.tensor_scalar(b, b, SC[0:NS, c0 + 14:c0 + 15], None, ALU.mult).then_inc(S["p_ok"], 1)
                    for e in (0, 1):
                        h = 2 * hp + e
                        ve.wait_ge(S["pt_mm"], l * 8 + h + 1)
                        if e:
                            ve.wait_ge(S["pv_mm"], l * 8 + h)
                        ve.tensor_copy(PT[:, 0:512], PS[:, 6, :])
                        ve.tensor_copy(PT[:, 512:896], PS[:, 7, 0:384])
                        ve.tensor_copy(PT[:, 1152:1280], PS[:, 7, 384:512]).then_inc(S["pt_d"], 1)
                    ve.wait_ge(S["pv_hi"], l * 4 + hp + 1)
                    o = (2 + hp) * T
                    tt(BL[:, o:o + NP_], PS[:, 1, 0:NP_], BH[:, o:o + NP_].bitcast(F32), ALU.subtract)
                    tt(BL[:, o + NP_:o + T], PS[:, 2, 0:NS], BH[:, o + NP_:o + T].bitcast(F32), ALU.subtract).then_inc(S["pv_lo"], 1)

                ve.wait_ge(S["pv_mm"], l * 8 + 8)
                X = LNT[5]
                EB, QD, KD, E = LNT[1:5]

                def blocks(ap, w):
                    return ap.rearrange("p (n t) -> p n t", t=w)
                tt(blocks(KD[:, 0:NP_], 128), blocks(B[:, 0:NP_], 128)[:, :, 127:128].to_broadcast([128, 4, 128]),
                   blocks(B[:, 0:NP_], 128), ALU.subtract)
                tt(KD[:, NP_:T], B[:, T - 1:T].to_broadcast([128, NS]), B[:, NP_:T], ALU.subtract)
                ve.drain().then_inc(S["kd_sub"], 1)
                ve.wait_ge(S["st_kr"], (l + 1) * 16)
                ve.memset(SB[:, :], 0.0)
                ve.memset(A[:, :], 0.0)
                ve.memset(AS[:, :], 0.0)
                ve.drain().then_inc(S["z_in"], 1)
                ve.wait_ge(S["eb_ok"], l + 1)
                tt(QD, GQ[:, :], EB, ALU.mult)
                ve.wait_ge(S["kdE"], l + 1)
                tt(KD, KD, GK[:, :], ALU.mult).then_inc(S["kd_ok"], 1)

                def lv_sub(j):
                    b = LEVELS[j]
                    w = NP_ if j < 2 else T
                    Bv, Ev = blocks(B[:, 0:w], 2 * b), blocks(E[:, 0:w], 2 * b)
                    ref = Bv[:, :, b - 1:b].to_broadcast([128, w // (2 * b), b])
                    tt(Ev[:, :, 0:b], ref, Bv[:, :, 0:b], ALU.subtract)
                    tt(Ev[:, :, b:2 * b], Bv[:, :, b:2 * b], ref, ALU.subtract)
                    ve.drain().then_inc(S["lv_e"], 1)

                lv_sub(0)
                group_done(l, "gv", 0, 1)
                ve.tensor_copy(VT[:, 0:1024].rearrange("p (b t) -> p b t", b=2), PS[:, 4:6, :])
                ve.tensor_copy(VT[0:NS, 1024:1280], PS[0:NS, 6, 0:256])
                ve.wait_ge(S["kdt_mm"], l + 1)
                ve.tensor_copy(KDT[:, 0:512], PS[:, 7, :])
                ve.tensor_copy(KDT[0:NS, 512:640], PS[0:NS, 3, 0:128]).then_inc(S["kdt_ok"], 1)

                def select(j, sample):
                    mk = MASK[:, j * 128:(j + 1) * 128]
                    for h in range(4):
                        if sample:
                            ve.copy_predicated(AS[0:NS, h * NS:(h + 1) * NS], mk[0:NS, 0:NS], PS[0:NS, 4 + h, 0:NS])
                        else:
                            ve.copy_predicated(blocks(A[:, h * NP_:(h + 1) * NP_], 128),
                                               mk.unsqueeze(1).to_broadcast([128, 4, 128]), blocks(PS[:, 4 + h, :], 128))

                for j in range(8):
                    n = l * KC + j
                    if j:
                        ve.wait_ge(S["lv_mm"], l * 8 + j)
                        settle(ve)
                        select(j - 1, False)
                        ve.drain().then_inc(S["lv_sel"], 1)
                    if j < 7:
                        b = LEVELS[j]
                        w = NP_ if j < 2 else T
                        ve.wait_ge(S["lv_E"], l * 7 + j + 1)
                        Xv, Ev = blocks(X[:, 0:w], 2 * b), blocks(E[:, 0:w], 2 * b)
                        tt(Xv[:, :, 0:b], Ev[:, :, 0:b], blocks(GK[:, 0:w], 2 * b)[:, :, 0:b], ALU.mult)
                        tt(Xv[:, :, b:2 * b], Ev[:, :, b:2 * b], blocks(GQ[:, 0:w], 2 * b)[:, :, b:2 * b], ALU.mult)
                        ve.drain().then_inc(S["lv_x"], 1)
                        if j < 6:
                            lv_sub(j + 1)
                    ve.wait_ge(S["pl_mm"], n + 1)
                    ve.wait_ge(S["ta_ok"], n + 1)
                    stt(two(LNT[3]), two(LNT[0]), 1.0, banks2(2), ALU.add, ALU.mult).then_inc(S["pl_rd"], 1)
                    if j == 0:
                        ve.wait_ge(S["ds_mm"], l + 1)
                        ve.wait_ge(S["gla_in"], (l + 1) * 64)
                        for i in range(5):
                            dst, src, eb = (i, i - 1, i * 128 + 127) if i < 4 else (5, 4, T - 1)
                            for h in range(4):
                                r = slice(32 * h, 32 * h + 32)
                                d = SB[r, dst * 256 + h * 64:dst * 256 + (h + 1) * 64]
                                o = (i % 2) * 256 + h * 64
                                inc = PS[r, 4 + i // 2, o:o + 64]
                                if i == 0:
                                    ve.tensor_copy(d, inc)
                                else:
                                    stt(d, SB[r, src * 256 + h * 64:src * 256 + (h + 1) * 64], EB[r, eb:eb + 1], inc,
                                        ALU.mult, ALU.add)
                            i_ = ve.drain()
                        i_.then_inc(S["sb_ok"], 1)
                    if j >= 2:
                        ve.wait_ge(S["smp_mm"], l * 6 + j - 1)
                        settle(ve)
                        select(j, True)
                        ve.drain().then_inc(S["smp_sel"], 1)
                    group_done(l, "ab", j, 1)
                    ve.wait_ge(S["tb_ok"], n + 1)
                    stt(two(MT[:, :]), two(LNT[1]), 1.0, banks2(0), ALU.add, ALU.mult).then_inc(S["ml_rd"], 1)
                    ve.drain()
                    tt(MIX[:, j * T:(j + 1) * T], LNT[3], MT[:, :], ALU.add)
                ve.wait_ge(S["lv_mm"], l * 8 + 8)
                settle(ve)
                select(7, False)
                ve.drain().then_inc(S["lv_sel"], 1)
                O3 = O[:, :].rearrange("p (c t) -> p c t", c=2)
                ve.wait_ge(S["o_mm"], l + 1)
                ve.tensor_copy(O3[:, :, 0:NP_], PS[:, 4:6, :])
                ve.tensor_copy(O3[:, :, NP_:T], PS[:, 6:8, 0:NS])
                ve.drain().then_inc(S["o_ok"], 1)
                ve.wait_ge(S["o_ms"], l + 1)
                ve.tensor_scalar(LN_[:, 2 * T:4 * T].rearrange("p (b t) -> p b t", b=4), PS[:, 4:8, 0:TH], 1.0 / 64, EPS,
                                 ALU.mult, ALU.add).then_inc(S["o_v"], 1)
                ve.wait_ge(S["o_r"], l + 1)
                stt(O[:, :], O[:, :], SMALL[:, SM_GN:SM_GN + 1], LN_[:, 2 * T:4 * T], ALU.mult, ALU.mult)
                ve.drain()
                stt(O[:, :], O[:, :], 0.5, SG[:, :], ALU.mult, ALU.mult).then_inc(S["o_y"], 1)
                ve.wait_ge(S["o_hi"], l + 1)
                tt(BL[:, 6 * T:8 * T], O[:, :], BH[:, 6 * T:8 * T].bitcast(F32), ALU.subtract).then_inc(S["o_lo"], 1)

                with ve.Fori(0, PAIRS["cg"]) as p:
                    for s in (0, 1):
                        m = p * 2 + s
                        group_done(l, "cg", p, s)
                        ve.wait_ge(S["tc_ok"], l * KC + m + 1)
                        x = bass.ds(m * T, T)
                        stt(two(LNT[s]), two(LNT[4 + s]), 1.0, banks2(4 + 2 * s), ALU.add, ALU.mult).then_inc(bank_free[s], 1)
                        ve.drain()
                        tt(LNT[s], LNT[s], MIX[:, x], ALU.add)
                        ve.drain().then_inc(S["m_ok"], 1)
                        ve.wait_ge(S["mx_hi"], l * KC + m + 1)
                        stt(MXL[:, x], LNT[s], 0.5, MXH[:, x].bitcast(F32), ALU.mult, ALU.subtract).then_inc(S["mx_lo"], 1)
                ve.wait_ge(S["mem_hi"], l + 1)
                tt(MML[:, :], MRAW[:, :], MMH[:, :].bitcast(F32), ALU.subtract).then_inc(S["mem_ready"], 1)
                proj_out(l, "wo", 4 * l + 1)
                ln_var(4 * l + 1)
                for p in range(4):
                    for s in (0, 1):
                        group_done(l, "memk", p, s)
                        o = (p * 2 + s) * NMEM
                        ve.tensor_copy(MK[0][:, o:o + NMEM], PS[:, 2 * s, 0:NMEM]).then_inc(bank_free[s], 1)
                    if p == 0:
                        ve.wait_ge(S["rstd"], 4 * l + 2)
                    for c in (2 * p, 2 * p + 1):
                        ln_chunk(c)
                for q in range(2):
                    for u in (0, 1):
                        group_done(l, "memv", q * 2 + u, 1)
                        for t in (0, 1):
                            o = (q * 2 + u) * 256 + t * D
                            i = ve.tensor_copy(MV[0][:, o:o + 256], PS[:, 2 * u, t * 256:(t + 1) * 256])
                        i.then_inc(bank_free[u], 1)

                def queries(h, s):
                    group_done(l, "cq", h, s)
                    ve.tensor_copy(two(LNT[s]), banks2(2 * s)).then_inc(bank_free[s], 1)
                for s in (0, 1):
                    queries(0, s)
                for h in range(4):
                    c0 = 16 * (h % 2)
                    ve.wait_ge(S["csc_mm"], l * 4 + h + 1)
                    ve.reduce_max(SC[:, c0:c0 + 4], PS[:, 4:6, :].rearrange("p b (i t) -> p (b i) t", i=2), AX.X)
                    ve.reduce_max(SC[0:NS, c0 + 4:c0 + 5], PS[0:NS, 6, 0:256], AX.X)
                    ve.drain()
                    ve.tensor_scalar(SC[:, c0 + 5:c0 + 10], SC[:, c0:c0 + 5], -MEM_SCALE, None, ALU.mult).then_inc(S["cmx_ok"], 1)
                    ve.wait_ge(S["cexp_ok"], l * 4 + h + 1)
                    ve.reciprocal(SC[:, c0 + 10:c0 + 15], SC[:, c0 + 10:c0 + 15])
                    ve.drain()
                    for i in range(4):
                        b = CP[h % 2][:, i * 256:(i + 1) * 256]
                        ve.tensor_scalar(b, b, SC[:, c0 + 10 + i:c0 + 11 + i], None, ALU.mult)
                    b = CP[h % 2][0:NS, 1024:1280]
                    ve.tensor_scalar(b, b, SC[0:NS, c0 + 14:c0 + 15], None, ALU.mult).then_inc(S["cp_ok"], 1)
                    if h < 3:
                        queries(h + 1, 0)
                    ve.wait_ge(S["cpt_mm"], l * 4 + h + 1)
                    ve.tensor_copy(CPT[:, 0:NP_], PS[:, 7, :])
                    ve.tensor_copy(CPT[:, T:T + NP_], PS[:, 4, :])
                    ve.tensor_copy(CPT[:, :].rearrange("p (k t) -> p k t", k=2)[:, :, NP_:T],
                                   PS[:, 6, 0:2 * NS].rearrange("p (k t) -> p k t", k=2)).then_inc(S["cpt_d"], 1)
                    if h < 3:
                        queries(h + 1, 1)
                    bp, bs = CPV[h]
                    for c in (0, 1):
                        ve.wait_ge(S["cpv_hi"], l * 8 + 2 * h + c + 1)
                        o = (2 * h + c) * T
                        if c == 0:
                            hi, lo_ = (x[:, o:o + 2 * T].rearrange("p (c t) -> p c t", c=2)[:, :, NP_:T] for x in (OH, OL))
                            tt(lo_, PS[:, bs, 0:2 * NS].rearrange("p (c t) -> p c t", c=2), hi.bitcast(F32), ALU.subtract)
                        tt(OL[:, o:o + NP_], PS[:, bp[c], 0:NP_], OH[:, o:o + NP_].bitcast(F32),
                           ALU.subtract).then_inc(S["cpv_lo"], 1)
                proj_out(l, "co", 4 * l + 2)
                layer_norm(4 * l + 2)

                ve.wait_ge(S["st_mem"], (l + 1) * 32)
                settle(ve)
                ffn_in(l, "f2i")
                ffn_out(l, "f2o", 4 * l + 3)


def tiles_of(w):
    l, k, m = w.shape
    return w.reshape(l, k // 128, 128, m // 128, 128).transpose(0, 3, 2, 1, 4)


def groups(w):
    t = tiles_of(w)
    return np.ascontiguousarray(t).reshape(t.shape[0], t.shape[1], 128, -1)


def feat(a):
    *lead, t, d = a.shape
    n = len(lead)
    a = a.reshape(*lead, t, d // 128, 128)
    return np.ascontiguousarray(a.transpose(*range(n), n + 2, n + 1, n)).reshape(*lead, 128, -1)


def unfeat(a, t):
    *lead, p, ct = a.shape
    n = len(lead)
    a = a.reshape(*lead, 128, ct // t, t)
    return np.ascontiguousarray(a.transpose(*range(n), n + 2, n + 1, n)).reshape(*lead, t, -1)


def constants():
    half = 16
    inv = (np.float32(10000.0) ** (-np.arange(half, dtype=np.float32) / np.float32(half))).astype(np.float32)
    pos = np.concatenate([np.arange(NP_), PAST + np.arange(NS)]).astype(np.float32)
    ang = (pos[None, :] * inv[:, None]).astype(np.float32)
    cos, sin = np.cos(ang), np.sin(ang)
    c2, s2 = np.concatenate([cos, cos]), np.concatenate([-sin, sin])
    one, zero = np.ones((64, T), np.float32), np.zeros((64, T), np.float32)
    reset = np.ones((128, T), np.float32)
    reset[:, 0::128] = 0
    tab = np.concatenate([np.concatenate([one, c2, s2]), np.concatenate([zero, c2, c2]),
                          np.concatenate([zero, s2, s2]), reset], 1).astype(np.float32)
    cst = np.zeros((128, 3 * 128 + 34), np.float32)
    cst[:, 0:128] = np.eye(128)
    cst[:, 128:256] = 1
    cst[0:64, 256:320] = 1
    cst[64:128, 320:384] = 1
    win = np.array([[2, 8], [4, 16]])
    for r in (0, 1):
        for c in (0, 1):
            cst[64 * r:64 * r + 64, 384 + 16 * c:400 + 16 * c] = 1.0 / np.minimum(np.arange(16) + 1, win[r, c])
            cst[64 * r:64 * r + 64, 416 + c] = 1.0 / win[r, c]
    s, t = np.meshgrid(np.arange(128), np.arange(128), indexing="ij")
    mask = [(s // (2 * b) == t // (2 * b)) & (s % (2 * b) < b) & (t % (2 * b) >= b) for b in LEVELS] + [s == t]
    mask = np.concatenate([m.astype(np.float32) for m in mask], 1)
    return tab, cst, np.ascontiguousarray(mask)


def layout(a):
    a = {k: np.asarray(v) for k, v in a.items()}
    f32 = np.float32
    d = {}
    d["x"] = feat(np.concatenate([a["x_prompt"][0], a["x_sample"][0]], 0))
    d["mem"] = feat(a["mem_prompt"][0])
    d["tab"], d["cst"], d["mask"] = constants()
    d["memk"] = groups(a["mem_w_k"])
    def moving(w, cols):
        l, k, m = w.shape
        return np.ascontiguousarray(w.reshape(l, k // 512, 4, 128, m // cols, cols).transpose(0, 4, 1, 3, 2, 5)).reshape(
            l, (m // cols) * (k // 512), 128, 4 * cols)
    d["memv"] = moving(a["mem_w_v"], 256)
    for n, wi, wo in (("f1", "w_ffn1_in", "w_ffn1_out"), ("f2", "w_ffn2_in", "w_ffn2_out")):
        t = groups(a[wi])
        d[n + "i"] = np.ascontiguousarray(t.reshape(L, 2, FC, 128, -1).transpose(0, 2, 1, 3, 4)).reshape(L, 2 * FC, 128, -1)
        t = tiles_of(a[wo])
        d[n + "o"] = np.ascontiguousarray(t.reshape(L, KC, 128, 2, 11, 128).transpose(0, 1, 3, 2, 4, 5)).reshape(
            L, 2 * KC, 128, -1)
    w = a["w_in"]
    cuts = np.cumsum([0, 256, 256, 256, 32, 128, 128, 256, 16, 256, 3072])
    pool, ql, ck, kr, gq, gk, gv, gate_in, gr, gates = (w[:, :, i:j] for i, j in zip(cuts, cuts[1:]))
    swap = np.concatenate([kr[:, :, 16:], kr[:, :, :16]], 2)
    z48, z64 = np.zeros((L, D, 48), f32), np.zeros((L, D, 64), f32)
    d["win"] = groups(np.concatenate([pool, ql, ck, gate_in, z48, kr, kr, z64, swap, swap, gq, gk, gr], 2))
    d["gv"] = moving(gv, 256)
    uq = a["mla_w_uq"].reshape(L, 256, 8, 96)
    uq = np.concatenate([uq[..., :64], uq[..., 64:], uq[..., 80:96], uq[..., 64:80]], -1).reshape(L, 256, 1024)
    uqt = tiles_of(uq)
    ukt = tiles_of(a["mla_w_uk"].reshape(L, 256, 512))
    q4 = uqt.reshape(L, 4, 2, 128, 256).transpose(0, 1, 3, 2, 4).reshape(L, 4, 128, 512)
    d["mla"] = np.ascontiguousarray(np.concatenate([q4, ukt.reshape(L, 4, 128, 256)], 3))
    d["vup"] = np.ascontiguousarray(a["mla_w_uv"].reshape(L, 2, 128, 512))
    g3 = groups(gates).reshape(L, 3, KC, 128, -1).transpose(0, 2, 1, 3, 4)
    b = groups(np.concatenate([a["w_branch_pool"], a["w_branch_mla"], a["w_branch_gla"]], 1))
    ga, gb, gc = g3[:, :, 0], g3[:, :, 1], g3[:, :, 2]
    d["ab"] = np.stack([np.concatenate([ga, b[..., 0:3 * 128]], -1), np.concatenate([gb, b[..., 3 * 128:6 * 128]], -1)],
                       2).reshape(L, 2 * KC, 128, -1)
    d["cg"] = np.concatenate([gc, b[..., 6 * 128:]], -1)
    d["wo"], d["cq"], d["co"] = groups(a["w_out"]), groups(a["mem_w_q"]), groups(a["mem_w_o"])

    sm = np.zeros((L, 128, SM_W), f32)
    sm[:, :, SM_LNG:SM_LNG + 32] = a["ln_g"].reshape(L, 32, 128).transpose(0, 2, 1)
    sm[:, :, SM_LNB:SM_LNB + 32] = a["ln_b"].reshape(L, 32, 128).transpose(0, 2, 1)
    for o, n in ((SM_PS, "pool_scale"), (SM_QN, "mla_q_norm"), (SM_KN, "mla_kv_norm")):
        sm[:, :, o:o + 2] = a[n].reshape(L, 2, 128).transpose(0, 2, 1)
    sm[:, :, SM_BA] = a["gla_b_a"]
    sm[:, :, SM_GN] = np.concatenate([a["gla_norm"], a["gla_norm"]], 1)
    for g in range(4):
        r = 64 * (g % 2)
        c = SM_PW + 128 * (g // 2) + r
        sm[:, r:r + 64, c:c + 64] = a["pool_w"][:, g]
    sm[:, 0:16, SM_WA:SM_WA + 128] = a["gla_w_a2"]
    d["small"] = sm
    d["pool_in"] = feat(a["cache_pool"][:, 0])
    d["ckv_in"] = feat(a["cache_mla_ckv"][:, 0])
    d["krope_in"] = np.ascontiguousarray(a["cache_mla_krope"][:, 0].transpose(0, 2, 1))
    d["gla_in"] = np.ascontiguousarray(a["state_gla"][:, 0].reshape(L, 128, 64))
    d["memk_in"] = feat(a["cache_mem_k"][:, 0].reshape(L, NMEM, D))
    d["memv_in"] = np.ascontiguousarray(a["cache_mem_v"][:, 0].reshape(L, 2, 128, D).transpose(0, 2, 1, 3)).reshape(L, 128, 2 * D)
    return d


OUTS = {"y": (128, KC * T), "pool_p": (L, 128, 2 * HIST), "pool_s": (L, 128, 2 * HIST), "ckv": (L, 128, 2 * T),
        "krope": (L, 32, T), "gla_p": (L, 128, 64), "gla_s": (L, 128, 64), "mem_k": (L, 128, KC * NMEM),
        "mem_v": (L, 128, 2 * D)}


def kernel(**inputs):
    import concourse.bacc as bacc
    from concourse.bass_utils import run_bass_kernel_spmd

    arrays = layout(inputs)
    nc = bacc.Bacc("TRN2", target_bir_lowering=False, num_devices=1)
    io = {}
    for n, v in arrays.items():
        io[n] = nc.dram_tensor("in_" + n, v.shape, mybir.dt.from_np(v.dtype), kind="ExternalInput").ap()
    for n, shape in OUTS.items():
        io[n] = nc.dram_tensor("out_" + n, shape, F32, kind="ExternalOutput").ap()
    build(nc, io)
    r = run_bass_kernel_spmd(nc, [{"in_" + n: v for n, v in arrays.items()}], core_ids=[0]).results[0]
    o = {n: np.asarray(r["out_" + n]) for n in OUTS}
    y = unfeat(o["y"], T)
    ckv = unfeat(o["ckv"], T)
    kr = o["krope"].transpose(0, 2, 1)
    mk = unfeat(o["mem_k"], NMEM).reshape(L, 1, NMEM, 4, 256)
    mv = np.ascontiguousarray(o["mem_v"].reshape(L, 128, 2, D).transpose(0, 2, 1, 3)).reshape(L, 1, NMEM, 4, 256)
    c = np.ascontiguousarray
    return (c(y[None, :NP_]), c(y[None, NP_:]),
            unfeat(o["pool_p"], HIST)[:, None], unfeat(o["pool_s"], HIST)[:, None],
            c(ckv[:, None, :NP_]), c(ckv[:, None, NP_:]), c(kr[:, None, :NP_]), c(kr[:, None, NP_:]),
            o["gla_p"].reshape(L, 1, 4, 32, 64), o["gla_s"].reshape(L, 1, 4, 32, 64), mk, mv)
```
